# Optimizing a Trainium2 kernel written in Bass

```python
import math
import jax, jax.numpy as jnp
from jax import lax
import numpy as np

D_MODEL = 1024
BATCH = 1
SEQ = 256
DEPTH = 2

GRID_W = 64
NA_HEAD_DIM = 64
NA_HEADS = (D_MODEL // 2) // NA_HEAD_DIM
NA_WIN_H_MAX = 8
NA_WIN_W = 16
NA_QBLOCK_W = 16
NA_KBLOCK_W = NA_QBLOCK_W + NA_WIN_W
ML_HEADS = 4
ML_HEAD_DIM = (D_MODEL // 2) // ML_HEADS
ML_CHUNK = 64
D_A = NA_HEADS * NA_HEAD_DIM
D_B = ML_HEADS * ML_HEAD_DIM
D_MIX = D_A + D_B
AB_IN = 3 * D_A + 4 * D_B + 4 * ML_HEADS
CONV_W = 3
D_FF = ((8 * D_MODEL // 3 + 255) // 256) * 256
N_EVEN = (DEPTH + 1) // 2
N_ODD = DEPTH // 2
DEEPNORM_ALPHA = (2 * DEPTH) ** 0.25
DEEPNORM_BETA = (8 * DEPTH) ** -0.25
LN_EPS = 1e-5

kernel_name = "hybrid_natten_mlstm_shortconv_macaron"

def layer_norm(x, g, b):
    xf = x.astype(jnp.float32)
    mu = jnp.mean(xf, axis=-1, keepdims=True)
    var = jnp.mean(jnp.square(xf - mu), axis=-1, keepdims=True)
    y = (xf - mu) * lax.rsqrt(var + LN_EPS)
    return (y * g.astype(jnp.float32) + b.astype(jnp.float32)).astype(x.dtype)

def swiglu_ffn(x, w_in, w_out):
    g, u = jnp.split(x @ w_in, 2, axis=-1)
    return (jax.nn.silu(g) * u) @ w_out

def neighbourhood_attention(q, k, v, rpb):
    B, S, H, dh = q.shape
    rows = S // GRID_W
    wh = min(NA_WIN_H_MAX, rows)
    nqb = GRID_W // NA_QBLOCK_W
    r = np.arange(rows)
    row_start = np.clip(r - wh // 2, 0, rows - wh)
    row_idx = row_start[:, None] + np.arange(wh)[None, :]
    c = np.arange(GRID_W)
    col_start = np.clip(c - NA_WIN_W // 2, 0, GRID_W - NA_WIN_W)
    kb_start = np.clip(np.arange(nqb) * NA_QBLOCK_W - NA_WIN_W // 2, 0, GRID_W - NA_KBLOCK_W)
    col_idx = kb_start[:, None] + np.arange(NA_KBLOCK_W)[None, :]
    qcol = c.reshape(nqb, NA_QBLOCK_W)
    qstart = col_start.reshape(nqb, NA_QBLOCK_W)[..., None]
    kcol = col_idx[:, None, :]
    col_ok = (kcol >= qstart) & (kcol < qstart + NA_WIN_W)
    dr = row_idx - r[:, None] + (NA_WIN_H_MAX - 1)
    dc = np.clip(kcol - qcol[..., None] + (NA_WIN_W - 1), 0, 2 * NA_WIN_W - 2)
    bias = rpb[:, dr[:, None, None, :, None], dc[None, :, :, None, :]]

    qg = q.reshape(B, rows, nqb, NA_QBLOCK_W, H, dh).transpose(0, 4, 1, 2, 3, 5)
    kg = k.reshape(B, rows, GRID_W, H, dh).transpose(0, 3, 1, 2, 4)
    vg = v.reshape(B, rows, GRID_W, H, dh).transpose(0, 3, 1, 2, 4)
    ri = row_idx[:, :, None, None]
    ci = col_idx[None, None, :, :]
    kb = kg[:, :, ri, ci]
    vb = vg[:, :, ri, ci]
    s = jnp.einsum('bhrjqd,bhrijkd->bhrjqik', qg, kb).astype(jnp.float32)
    s = s + bias.astype(jnp.float32)[None]
    s = jnp.where(col_ok[:, :, None, :], s, -jnp.inf)
    p = jax.nn.softmax(s, axis=(-2, -1)).astype(v.dtype)
    o = jnp.einsum('bhrjqik,bhrijkd->bhrjqd', p, vb)
    return o.transpose(0, 2, 3, 4, 1, 5).reshape(B, S, H * dh)

def mlstm_chunkwise(q, k, v, i_pre, f_pre):
    B, H, S, d = q.shape
    L = ML_CHUNK
    nc = S // L
    logf = jax.nn.log_sigmoid(f_pre)

    def to_chunks(a):
        return jnp.moveaxis(a.reshape(B, H, nc, L, *a.shape[3:]), 2, 0)

    xs = (to_chunks(q), to_chunks(k), to_chunks(v), to_chunks(i_pre), to_chunks(logf))
    lower = jnp.asarray(np.tril(np.ones((L, L), dtype=bool)))

    def step(carry, xs_c):
        C, n, m = carry
        qx, kx, vx, ix, fx = xs_c
        b = jnp.cumsum(fx, axis=-1)
        g = b[..., -1]
        dmat = jnp.where(lower, b[..., :, None] - b[..., None, :] + ix[..., None, :], -jnp.inf)
        inter = b + m[..., None]
        m_t = jnp.maximum(inter, jnp.max(dmat, axis=-1))
        w = jnp.exp(dmat - m_t[..., None])
        s_inter = jnp.exp(inter - m_t)
        qk = jnp.einsum('bhtd,bhsd->bhts', qx, kx) * w
        num = jnp.einsum('bhts,bhse->bhte', qk, vx) + s_inter[..., None] * jnp.einsum('bhtd,bhde->bhte', qx, C)
        den = jnp.sum(qk, axis=-1) + s_inter * jnp.einsum('bhtd,bhd->bht', qx, n)
        h = num / jnp.maximum(jnp.abs(den), jnp.exp(-m_t))[..., None]
        a = g[..., None] - b + ix
        m_new = jnp.maximum(g + m, jnp.max(a, axis=-1))
        decay = jnp.exp(g + m - m_new)
        wa = jnp.exp(a - m_new[..., None])
        C_new = decay[..., None, None] * C + jnp.einsum('bhs,bhsd,bhse->bhde', wa, kx, vx)
        n_new = decay[..., None] * n + jnp.einsum('bhs,bhsd->bhd', wa, kx)
        return (C_new, n_new, m_new), h

    init = (jnp.zeros((B, H, d, d), jnp.float32), jnp.zeros((B, H, d), jnp.float32),
            jnp.zeros((B, H), jnp.float32))
    _, hs = lax.scan(step, init, xs)
    return jnp.moveaxis(hs, 0, 2).reshape(B, H, S, d)

def na_mlstm_mixer(x, w_in, gate_b, rpb, gn_g, w_out):
    B, S, _ = x.shape
    cuts = [D_A, 2 * D_A, 3 * D_A, 3 * D_A + D_B, 3 * D_A + 2 * D_B, 3 * D_A + 3 * D_B, 3 * D_A + 4 * D_B]
    qa, ka, va, qb, kb, vb, ob, gates = jnp.split(x @ w_in, cuts, axis=-1)
    ha = lambda t: t.reshape(B, S, NA_HEADS, NA_HEAD_DIM)
    ya = neighbourhood_attention(ha(qa) * (NA_HEAD_DIM ** -0.5), ha(ka), ha(va), rpb)
    hb = lambda t: t.reshape(B, S, ML_HEADS, ML_HEAD_DIM).transpose(0, 2, 1, 3).astype(jnp.float32)
    q_m, k_m, v_m = hb(qb), hb(kb) * (ML_HEAD_DIM ** -0.5), hb(vb)
    g = gates.astype(jnp.float32).reshape(B, S, 4, ML_HEADS) + gate_b.astype(jnp.float32)
    i_f, f_f, i_b, f_b = g.transpose(2, 0, 3, 1)
    h_fwd = mlstm_chunkwise(q_m, k_m, v_m, i_f, f_f)
    flip = lambda t: jnp.flip(t, axis=2)
    h_bwd = flip(mlstm_chunkwise(flip(q_m), flip(k_m), flip(v_m), flip(i_b), flip(f_b)))
    h = h_fwd + h_bwd
    mu = jnp.mean(h, axis=-1, keepdims=True)
    var = jnp.mean(jnp.square(h - mu), axis=-1, keepdims=True)
    hn = ((h - mu) * lax.rsqrt(var + LN_EPS)).transpose(0, 2, 1, 3).reshape(B, S, D_B)
    yb = (jax.nn.sigmoid(ob.astype(jnp.float32)) * hn * gn_g.astype(jnp.float32)).astype(x.dtype)
    return jnp.concatenate([ya, yb], axis=-1) @ w_out

def short_conv_mixer(x, w_in, conv_w, conv_b, w_out):
    bg, cg, h = jnp.split(x @ w_in, 3, axis=-1)
    u = cg * h
    y = lax.conv_general_dilated(u, conv_w[:, None, :].astype(u.dtype), window_strides=(1,),
                                 padding=((CONV_W // 2, CONV_W // 2),),
                                 dimension_numbers=('NWC', 'WIO', 'NWC'),
                                 feature_group_count=D_MODEL) + conv_b
    return (bg * y) @ w_out

def setup_inputs(seed: int = 0) -> dict:
    key = jax.random.key(seed)
    ks = jax.random.split(key, 16)
    nrm = jax.random.normal
    x = nrm(ks[0], (BATCH, SEQ, D_MODEL), jnp.float32)
    ln_g = 1.0 + 0.02 * nrm(ks[1], (DEPTH, 3, D_MODEL), jnp.float32)
    ln_b = 0.02 * nrm(ks[2], (DEPTH, 3, D_MODEL), jnp.float32)
    ffn_w_in = nrm(ks[3], (DEPTH, 2, D_MODEL, 2 * D_FF), jnp.float32) * D_MODEL ** -0.5
    ffn_w_out = nrm(ks[4], (DEPTH, 2, D_FF, D_MODEL), jnp.float32) * (D_FF ** -0.5 * DEEPNORM_BETA)
    ab_w_in = nrm(ks[5], (N_EVEN, D_MODEL, AB_IN), jnp.float32) * D_MODEL ** -0.5
    f_bias = jnp.linspace(3.0, 6.0, ML_HEADS, dtype=jnp.float32)
    zero_h = jnp.zeros((ML_HEADS,), jnp.float32)
    ab_gate_b = jnp.stack([zero_h, f_bias, zero_h, f_bias])[None] + 0.1 * nrm(ks[6], (N_EVEN, 4, ML_HEADS), jnp.float32)
    na_rpb = 0.02 * nrm(ks[7], (N_EVEN, NA_HEADS, 2 * NA_WIN_H_MAX - 1, 2 * NA_WIN_W - 1), jnp.float32)
    ml_gn_g = 1.0 + 0.02 * nrm(ks[8], (N_EVEN, D_B), jnp.float32)
    ab_w_out = nrm(ks[9], (N_EVEN, D_MIX, D_MODEL), jnp.float32) * (D_MIX ** -0.5 * DEEPNORM_BETA)
    sc_w_in = nrm(ks[10], (N_ODD, D_MODEL, 3 * D_MODEL), jnp.float32) * D_MODEL ** -0.5
    sc_conv_w = nrm(ks[11], (N_ODD, CONV_W, D_MODEL), jnp.float32) * CONV_W ** -0.5
    sc_conv_b = 0.02 * nrm(ks[12], (N_ODD, D_MODEL), jnp.float32)
    sc_w_out = nrm(ks[13], (N_ODD, D_MODEL, D_MODEL), jnp.float32) * (D_MODEL ** -0.5 * DEEPNORM_BETA)
    return {"x": x, "ln_g": ln_g, "ln_b": ln_b, "ffn_w_in": ffn_w_in, "ffn_w_out": ffn_w_out,
            "ab_w_in": ab_w_in, "ab_gate_b": ab_gate_b, "na_rpb": na_rpb, "ml_gn_g": ml_gn_g,
            "ab_w_out": ab_w_out, "sc_w_in": sc_w_in, "sc_conv_w": sc_conv_w,
            "sc_conv_b": sc_conv_b, "sc_w_out": sc_w_out}

def reference(x, ln_g, ln_b, ffn_w_in, ffn_w_out, ab_w_in, ab_gate_b, na_rpb, ml_gn_g,
              ab_w_out, sc_w_in, sc_conv_w, sc_conv_b, sc_w_out):
    a = DEEPNORM_ALPHA
    for layer in range(DEPTH):
        x = layer_norm(a * x + 0.5 * swiglu_ffn(x, ffn_w_in[layer, 0], ffn_w_out[layer, 0]),
                       ln_g[layer, 0], ln_b[layer, 0])
        if layer % 2 == 0:
            e = layer // 2
            mix = na_mlstm_mixer(x, ab_w_in[e], ab_gate_b[e], na_rpb[e], ml_gn_g[e], ab_w_out[e])
        else:
            o = layer // 2
            mix = short_conv_mixer(x, sc_w_in[o], sc_conv_w[o], sc_conv_b[o], sc_w_out[o])
        x = layer_norm(a * x + mix, ln_g[layer, 1], ln_b[layer, 1])
        x = layer_norm(a * x + 0.5 * swiglu_ffn(x, ffn_w_in[layer, 1], ffn_w_out[layer, 1]),
                       ln_g[layer, 2], ln_b[layer, 2])
    return x


_drawn_inputs = setup_inputs


def setup_inputs(seed=0):
    import zlib

    import numpy as np

    out = dict(_drawn_inputs(seed))
    spreads = {}
    factors = {'na_rpb': 8.0, 'ml_gn_g': 8.0, 'sc_conv_b': 8.0}
    for name, (base, spread) in spreads.items():
        noise = np.random.default_rng([zlib.crc32(name.encode()), seed]).standard_normal(out[name].shape)
        drawn = base * np.exp(spread * noise) if base else spread * noise
        out[name] = __import__('jax').numpy.asarray(drawn.astype(out[name].dtype))
    for name, factor in factors.items():
        out[name] = (out[name] * factor).astype(out[name].dtype)
    return out
```

```python
from contextlib import ExitStack

import numpy as np

import concourse.bass as bass
from concourse import mybir

ALU = mybir.AluOpType
ACT = mybir.ActivationFunctionType
F32 = mybir.dt.float32
F32R = mybir.dt.float32r

P = 128
D = 1024
S = 256
NT = S // P
KB = D // P
FF = 2816
FKB = FF // P
FSTEPS = FF // 256
HALF_D = D // 2
NA_H, NA_D = 8, 64
ML_H, ML_D = 4, 128
GRID_W, WIN_W = 64, 16
ROWS = S // GRID_W
RPB_R, RPB_C = 15, 31
N_GATES = 4 * ML_H
ALPHA = 4.0 ** 0.25
EPS = 1e-5
NEG = -1e30

RING = 4
TILES = 4
LEAD = 3
FILL = 16

FFN, MIX, CONV = "ffn", "mix", "conv"
MIX_COLS = ["vb", "qb", "kb", "ob", "va", "qa", "ka"]
MIX_AT = {n: i for i, n in enumerate(["qa", "ka", "va", "qb", "kb", "vb", "ob"])}
TRANSPOSED = ("qb", "kb", "qa", "ka")
PHASES = [(FFN, FSTEPS, FKB), (MIX, len(MIX_COLS), KB), (FFN, FSTEPS, FKB),
          (FFN, FSTEPS, FKB), (CONV, 3 * D // 512, KB), (FFN, FSTEPS, FKB)]
CONV_STEPS = [(1, 0), (2, 0), (0, 0), (1, 1), (2, 1), (0, 1)]

USED = []
GROUP0, STEP0, BATCH0 = [], [], []
KINDS = ["lo"] * 4
_g = _n = 0
for _kind, _steps, _kb in PHASES:
    GROUP0.append(_g)
    STEP0.append(_n)
    BATCH0.append(len(KINDS))
    _g += 2 * _steps + _kb // 2
    _n += _steps
    KINDS += {FFN: ["lo"] * FSTEPS, MIX: ["pt"] * ML_H + ["lo"] * 2 + ["pt"] * NA_H, CONV: []}[_kind]
    for _i in range(_steps):
        USED += [("group", sum(u[0] == "group" for u in USED) + 1), ("proj", 2 * (STEP0[-1] + _i) + 2)]
    for _i in range(_kb // 2 - 1):
        USED.append(("group", sum(u[0] == "group" for u in USED) + 1))
    USED.append(("acc", 2 * len(GROUP0)))
    KINDS += ["lo"] * 4
GROUPS = _g
LAST = len(PHASES) - 1


def kind_count(m):
    return sum(k == KINDS[m] for k in KINDS[:m + 1])


def x_batch(phase):
    return 0 if phase == 0 else BATCH0[phase] + 0 - 4


def acc_pair(phase):
    return (STEP0[phase] + PHASES[phase][1]) % 2


def constants():
    s = np.arange(P)[:, None]
    t = np.arange(P)[None, :]
    cols = [np.eye(P), s <= t, s >= t, np.ones((P, P)),
            np.zeros((P, P)), np.where(t <= s, 0, NEG),
            np.where(t >= s, 0, NEG), np.zeros((P, P))]
    c = np.arange(P)[:, None] % GRID_W
    kc = np.arange(GRID_W)[None, :]
    start = np.clip(c - WIN_W // 2, 0, GRID_W - WIN_W)
    cols.append(np.where((kc >= start) & (kc < start + WIN_W), 0, NEG)[:, ::-1])
    return np.concatenate([np.asarray(a, np.float32) for a in cols], axis=1)


def allowed(d, t):
    return (0, S) if t != d else (t * P, (t + 1) * P)


def mask_start(d, t):
    return P if (d, t) == (0, 0) else 0


CONST_W = 8 * P + GRID_W


def build(nc, x, ln_g, ln_b, ab_gate_b, na_rpb, ml_gn_g, weights, gate_w, conv_taps, consts, out):
    ctx = ExitStack()
    with ctx:
        def sem(name):
            return ctx.enter_context(nc.semaphore(name))

        def sb(name, shape, dt=F32):
            return ctx.enter_context(nc.sbuf_tensor(name, shape, dt))

        raw = sb("raw", [P, RING, TILES * 512])
        w_hi = sb("w_hi", [P, RING, TILES * 512], F32R)
        w_lo = sb("w_lo", [P, RING, TILES * 512], F32R)
        xs = sb("xs", [P, NT, D])
        ax = sb("ax", [P, NT, D])
        xT_hi = sb("xT_hi", [P, KB, S], F32R)
        xT_lo = sb("xT_lo", [P, KB, S], F32R)
        gb = sb("gb", [P, 2, D])
        cst = sb("cst", [P, CONST_W])
        wg = sb("wg", [P, KB, N_GATES])
        wg_hi = sb("wg_hi", [P, KB, N_GATES], F32R)
        wg_lo = sb("wg_lo", [P, KB, N_GATES], F32R)
        gate_bias = sb("gate_bias", [P, N_GATES])
        stats = sb("stats", [P, 2, 6])
        mv = sb("mv", [P, NT, 2])
        var_eps = sb("var_eps", [P, 8])
        rstd = sb("rstd", [P, 8])
        minus_half = sb("minus_half", [P, 8])
        small = sb("small", [P, 16, 16])
        ident = cst[:, 0:P]
        tri_f = cst[:, P:2 * P]
        tri_b = cst[:, 2 * P:3 * P]
        ones = cst[:, 3 * P:4 * P]
        mask_f = cst[:, 4 * P:6 * P]
        mask_b = cst[:, 6 * P:8 * P]
        mask_na = cst[:, 8 * P:8 * P + GRID_W]

        ARENA = 63488
        arena_at = -(-nc.sbuf_base // 32) * 32
        sb("arena", [P, ARENA // 4])
        at = {}

        def place(phase, name, shape, dt=F32):
            size = int(np.prod(shape[1:])) * 4
            offset = at.get(phase, 0)
            at[phase] = offset + size
            assert at[phase] <= ARENA, (phase, name, at[phase])
            return nc.alloc_sbuf_tensor_at(name, shape, dt, offset=arena_at + offset)

        hT_hi = place(FFN, "hT_hi", [P, FKB, S], F32R)
        hT_lo = place(FFN, "hT_lo", [P, FKB, S], F32R)
        hid = place(FFN, "hid", [P, 2, NT, 256])

        score = place(MIX, "score", [P, ML_H, 2, NT, S])
        ybT_hi = place(MIX, "ybT_hi", [P, 4, S], F32R)
        ybT_lo = place(MIX, "ybT_lo", [P, 4, S], F32R)
        qT = place(MIX, "qT", [P, 4, S])
        kT = place(MIX, "kT", [P, 4, S])
        v_ml = place(MIX, "v_ml", [P, NT, 512])
        o_gate = place(MIX, "o_gate", [P, NT, 512])
        v_na = place(MIX, "v_na", [P, NT, 512])
        pT = place(MIX, "pT", [P, 2, NT, S])
        rpb = place(MIX, "rpb", [P, NA_H, 6, GRID_W])
        yaT_hi = nc.alloc_sbuf_tensor_at("yaT_hi", [P, 4, S], F32R, offset=arena_at)
        yaT_lo = nc.alloc_sbuf_tensor_at("yaT_lo", [P, 4, S], F32R, offset=arena_at + 4096)
        gn_gain = place(MIX, "gn_gain", [P, 512])
        h_ml = xs[:, :, 0:512]
        na_s = xs[:, :, 512:1024]

        cgT = place(CONV, "cgT", [P, 4, S])
        uT = place(CONV, "uT", [P, 4, S + 2])
        yT = place(CONV, "yT", [P, 4, S])
        zT = place(CONV, "zT", [P, 4, S])
        zT_hi = place(CONV, "zT_hi", [P, KB, S], F32R)
        zT_lo = place(CONV, "zT_lo", [P, KB, S], F32R)
        taps = sb("taps", [P, KB, 4])

        psum = ctx.enter_context(nc.psum_tensor("psum", [P, 8, 512], F32))

        def pair(p):
            return psum[:, 2 * p:2 * p + 2, :]

        raw_in = [sem(f"raw_in{i}") for i in range(RING)]
        hi_made = sem("hi_made")
        lo_made = sem("lo_made")
        group_used = sem("group_used")
        proj_ready = sem("proj_ready")
        proj_saved = sem("proj_saved")
        conv_read = sem("conv_read")
        silu_ready = sem("silu_ready")
        hid_ready = sem("hid_ready")
        tp_ready = sem("tp_ready")
        tp_hi = sem("tp_hi")
        tp_lo = sem("tp_lo")
        pt_saved = sem("pt_saved")
        acc_ready = sem("acc_ready")
        x_ready = sem("x_ready")
        ax_ready = sem("ax_ready")
        var_ready = sem("var_ready")
        rstd_ready = sem("rstd_ready")
        v_step = sem("v_step")
        p_step = sem("p_step")
        x_in = [sem(f"x_in{t}") for t in range(NT)]
        ident_in = sem("ident_in")
        cst_in = sem("cst_in")
        gb_in = sem("gb_in")
        wg_in = sem("wg_in")
        wg_split = sem("wg_split")
        rpb_in = sem("rpb_in")
        rpb_made = sem("rpb_made")
        gates_ready = sem("gates_ready")
        gate_v = sem("gate_v")
        gate_a = sem("gate_a")
        cum_ready = sem("cum_ready")
        row_ready = sem("row_ready")
        ml_s_ready = sem("ml_s_ready")
        ml_free = sem("ml_free")
        max_ready = sem("max_ready")
        ml_w_ready = sem("ml_w_ready")
        ml_p_ready = sem("ml_p_ready")
        ml_h_ready = sem("ml_h_ready")
        ml_h_saved = sem("ml_h_saved")
        yb_ready = sem("yb_ready")
        gn_in = sem("gn_in")
        na_s_ready = sem("na_s_ready")
        na_max = sem("na_max")
        na_exp = sem("na_exp")
        na_p = sem("na_p")
        na_o_ready = sem("na_o_ready")
        ya_hi = sem("ya_hi")
        ya_lo = sem("ya_lo")
        taps_in = sem("taps_in")
        z_hi = sem("z_hi")
        z_lo = sem("z_lo")
        out_done = sem("out_done")

        block = ctx.enter_context(nc.Block())

        def batch_bank(m):
            return psum[:, 4 + m % 2, :]

        def wait_batch_bank(e, m):
            if m >= 2:
                e.wait_ge(tp_lo if KINDS[m - 2] == "lo" else pt_saved, kind_count(m - 2))

        @block.sync
        def _(sp):
            sp.dma_start(xs[:, 0, :], x[0, 0:P, :]).then_inc(x_in[0], 16)

            def fill(g, slot):
                if not isinstance(g, int) or g >= RING:
                    sp.wait_ge(lo_made, g - RING + 1)
                sp.dma_start(raw[:, slot, :], weights[bass.ds(g * P, P), :]).then_inc(raw_in[slot], FILL)

            fill(0, 0)
            fill(1, 1)
            sp.dma_start(xs[:, 1, :], x[0, P:S, :]).then_inc(x_in[1], 16)
            fill(2, 2)
            fill(3, 3)
            with sp.Fori(1, GROUPS // RING) as it:
                for slot in range(RING):
                    fill(it * RING + slot, slot)
            for g in range(GROUPS // RING * RING, GROUPS):
                fill(g, g % RING)

            for t in range(NT):
                for c in range(2):
                    sp.wait_ge(x_ready, 4 * LAST + 2 * t + c + 1)
                    sp.dma_start(out[0, t * P:(t + 1) * P, c * 512:(c + 1) * 512],
                                 xs[:, t, c * 512:(c + 1) * 512]).then_inc(out_done, 16)
            sp.wait_ge(out_done, 16 * 4)

        @block.gpsimd
        def _(pool):
            pool.dma_start(ident, consts[:, 0:P]).then_inc(ident_in, 16)
            nc.gpsimd.memset(minus_half[:, :], -0.5).then_inc(p_step, 1)
            pool.wait_ge(lo_made, 4)
            pool.dma_start(cst[:, P:], consts[:, P:]).then_inc(cst_in, 16)
            pool.dma_start(wg[:, :, :], gate_w).then_inc(wg_in, 16)
            pool.dma_start(gate_bias[:, :],
                           ab_gate_b[0].rearrange("a h -> (a h)").partition_broadcast(P)).then_inc(wg_in, 16)
            pool.dma_start(taps[:, :, :], conv_taps).then_inc(taps_in, 16)
            pool.wait_ge(p_step, 1)
            done = 0

            def rsqrt(n):
                nonlocal done
                done += 1
                pool.wait_ge(var_ready, done)
                nc.gpsimd.tensor_tensor(rstd[:, 0:n], var_eps[:, 0:n], minus_half[:, 0:n],
                                        ALU.pow).then_inc(rstd_ready, 1)

            for phase, (kind, _, _) in enumerate(PHASES):
                if phase:
                    pool.wait_ge(x_ready, 4 * phase)
                layer, i = divmod(phase, 3)
                for j, v in enumerate((ln_g, ln_b)):
                    pool.dma_start(gb[:, j, :], v[layer, i, :].partition_broadcast(P)).then_inc(gb_in, 16)
                if kind == MIX:
                    pool.wait_ge(acc_ready, 2 * phase)
                    for r2 in range(2):
                        for j in range(6):
                            first = (5 - r2 + j) * RPB_C + RPB_C // 2 - (GRID_W - 1)
                            pool.dma_start(rpb[64 * r2:64 * r2 + 64, :, j, :],
                                           bass.AP(na_rpb.tensor, first,
                                                   [[1, 64], [RPB_R * RPB_C, NA_H], [1, GRID_W]])
                                           ).then_inc(rpb_in, 16)
                    pool.dma_start(gn_gain[:, :], ml_gn_g[0].partition_broadcast(P)).then_inc(gn_in, 16)
                    pool.wait_ge(rpb_in, 16 * 12)
                    pool.wait_ge(cst_in, 16)
                    v = rpb[:, :, :, :].rearrange("p h j c -> p (h j) c")
                    nc.gpsimd.tensor_tensor(v, v, mask_na.unsqueeze(1).to_broadcast([P, NA_H * 6, GRID_W]),
                                            ALU.add).then_inc(rpb_made, 1)
                    rsqrt(8)
                for t in range(NT):
                    rsqrt(1)

        @block.tensor
        def _(pe):
            mm = nc.tensor.matmul

            def split_mm(ps, s_hi, s_lo, m_hi, m_lo, first, last):
                mm(ps, s_hi, m_hi, start=first, stop=False)
                mm(ps, s_hi, m_lo, start=False, stop=False)
                return mm(ps, s_lo, m_hi, start=False, stop=last)

            def tile(slot, i):
                return w_hi[:, slot, i * 512:(i + 1) * 512], w_lo[:, slot, i * 512:(i + 1) * 512]

            def transposes(m, blocks):
                for i, b in enumerate(blocks):
                    last = nc.tensor.transpose(batch_bank(m)[:, i * P:(i + 1) * P], b, ident)
                last.then_inc(tp_ready, 1)

            def x_transposes(phase, t):
                for c in range(2):
                    m = x_batch(phase) + 2 * t + c
                    if phase == 0:
                        pe.wait_ge(x_in[t], 16)
                        pe.wait_ge(ident_in, 16)
                    else:
                        pe.wait_ge(x_ready, 4 * (phase - 1) + 2 * t + c + 1)
                    wait_batch_bank(pe, m)
                    transposes(m, [xs[:, t, (4 * c + k) * P:(4 * c + k + 1) * P] for k in range(4)])


            def natural_step(par, slots, g, between=None):
                for t in range(NT):
                    for k in range(KB):
                        if t == 0 and k % 4 == 0:
                            pe.wait_ge(lo_made, g + 1 + k // 4)
                        hi, lo = tile(slots[k // 4], k % 4)
                        tok = slice(t * P, (t + 1) * P)
                        last = split_mm(pair(par)[:, t, :], xT_hi[:, k, tok], xT_lo[:, k, tok],
                                        hi, lo, k == 0, k == KB - 1)
                        if t == 1 and k == 3:
                            last.then_inc(group_used, 1)
                    if t == 0:
                        last.then_inc(proj_ready, 1)
                        if between:
                            between()
                return last

            def x_half(phase, t):
                x_transposes(phase, t)
                pe.wait_ge(tp_lo, kind_count(x_batch(phase) + 2 * t + 1))

            def transposed_step(par, slots, g):
                pe.wait_ge(lo_made, g + 2)
                for b in range(4):
                    for k in range(KB):
                        hi, lo = tile(slots[k // 4], k % 4)
                        blk = slice(b * P, (b + 1) * P)
                        ps = pair(par)[:, b // 2, (b % 2) * S:(b % 2 + 1) * S]
                        mm(ps, hi[:, blk], xT_hi[:, k, :], start=k == 0, stop=False)
                        mm(ps, hi[:, blk], xT_lo[:, k, :], start=False, stop=False)
                        last = mm(ps, lo[:, blk], xT_hi[:, k, :], start=False, stop=k == KB - 1)
                        if b == 3 and k == 3:
                            last.then_inc(group_used, 1)
                    if b == 1:
                        last.then_inc(proj_ready, 1)
                return last

            def output(phase, hi, lo, wait_pair, wait_blocks, after_first=None):
                g0 = GROUP0[phase] + 2 * PHASES[phase][1]
                n_groups = PHASES[phase][2] // 2
                banks = [pair(acc_pair(phase)), psum[:, 6:8, :]]

                def block_mm(j, kk, t, kb_last):
                    kb = 2 * j + kk
                    slot = (g0 + j) % RING
                    tok = slice(t * P, (t + 1) * P)
                    for c in range(2):
                        w1, w2 = tile(slot, 2 * kk + c)
                        last = split_mm(banks[t][:, c, :], hi(kb)[:, tok], lo(kb)[:, tok], w1, w2,
                                        kb == 0, kb == kb_last)
                    return last

                kb_last = 2 * n_groups - 1
                wait_pair()
                for j in range(n_groups - 2):
                    pe.wait_ge(lo_made, g0 + j + 1)
                    wait_blocks(j)
                    for kk in range(2):
                        for t in range(NT):
                            last = block_mm(j, kk, t, kb_last)
                    last.then_inc(group_used, 1)
                    if j == 0 and after_first:
                        after_first()
                pe.wait_ge(lo_made, g0 + n_groups)
                for t in range(NT):
                    for j in range(n_groups - 2, n_groups):
                        if t == 0:
                            wait_blocks(j)
                        for kk in range(2):
                            last = block_mm(j, kk, t, kb_last)
                        if t == 1 and j == n_groups - 2:
                            last.then_inc(group_used, 1)
                    last.then_inc(acc_ready, 1)

            def ffn(phase):
                g0, n0, m0 = GROUP0[phase], STEP0[phase], BATCH0[phase]
                h0 = sum(k == FFN for k, _, _ in PHASES[:phase]) * FSTEPS

                def hid_transposes(par, h_count, m_wait, bank):
                    pe.wait_ge(hid_ready, h_count)
                    pe.wait_ge(tp_lo, m_wait)
                    for i in range(4):
                        kk, t = divmod(i, 2)
                        last = nc.tensor.transpose(psum[:, 4 + bank, i * P:(i + 1) * P],
                                                   hid[:, par, t, kk * P:(kk + 1) * P], ident)
                    last.then_inc(tp_ready, 1)

                def step(s, off=0):
                    par = (n0 + off) % 2
                    g = s * 2 + (g0 + 2 * off)
                    slots = [(g0 + 2 * off) % RING, (g0 + 2 * off + 1) % RING]
                    first = isinstance(s, int) and s + off == 0
                    if not isinstance(s, int) or s + off >= 2:
                        pe.wait_ge(hid_ready, s + (h0 + off - 1))

                    def between():
                        lo0 = kind_count(m0) - 1
                        hid_transposes((off + 1) % 2, s + (h0 + off), s + (lo0 + off - 2),
                                       (m0 + off - 1) % 2)
                    natural_step(par, slots, g, (lambda: x_half(phase, 1)) if first else between
                                 ).then_inc(proj_ready, 1)

                x_half(phase, 0)
                step(0, 0)
                step(0, 1)
                with pe.Fori(1, (FSTEPS - 1) // 2) as it:
                    for off in range(2):
                        step(it * 2, off)
                step(FSTEPS - 1, 0)
                lo0 = kind_count(m0)

                def last_transposes():
                    s = FSTEPS
                    hid_transposes((s + 1) % 2, h0 + s, lo0 + s - 3, (m0 + s - 1) % 2)

                output(phase, lambda kb: hT_hi[:, kb, :], lambda kb: hT_lo[:, kb, :],
                       lambda: pe.wait_ge(hid_ready, h0 + FSTEPS - 1), lambda j: pe.wait_ge(tp_lo, lo0 + j), last_transposes)

            def mix(phase):
                g0, n0, m0 = GROUP0[phase], STEP0[phase], BATCH0[phase]

                def step(i, *between):
                    if i >= 2:
                        pe.wait_ge(proj_saved, i - 1)
                    slots = [(g0 + 2 * i) % RING, (g0 + 2 * i + 1) % RING]
                    f = transposed_step if MIX_COLS[i] in TRANSPOSED else natural_step
                    f((n0 + i) % 2, slots, g0 + 2 * i, *between).then_inc(proj_ready, 1)

                def gates():
                    x_half(phase, 1)
                    pe.wait_ge(wg_split, 2)
                    for t in range(NT):
                        tok = slice(t * P, (t + 1) * P)
                        for k in range(KB):
                            last = split_mm(psum[:, 4, t * N_GATES:(t + 1) * N_GATES], xT_hi[:, k, tok],
                                            xT_lo[:, k, tok], wg_hi[:, k, :], wg_lo[:, k, :],
                                            k == 0, k == KB - 1)
                    last.then_inc(gates_ready, 1)

                x_half(phase, 0)
                step(0, gates)

                pe.wait_ge(gate_v, 2)
                pe.wait_ge(cst_in, 16)
                cum = psum[:, 5, 0:16].rearrange("p (t d h) -> p t d h", t=2, d=2)
                lf = small[:, 0, :].rearrange("p (t d h) -> p t d h", t=2, d=2)
                mm(cum[:, 0, 0, :], tri_f, lf[:, 0, 0, :], start=True, stop=True)
                mm(cum[:, 1, 0, :], ones, lf[:, 0, 0, :], start=True, stop=False)
                mm(cum[:, 1, 0, :], tri_f, lf[:, 1, 0, :], start=False, stop=True)
                mm(cum[:, 1, 1, :], tri_b, lf[:, 1, 1, :], start=True, stop=True)
                mm(cum[:, 0, 1, :], ones, lf[:, 1, 1, :], start=True, stop=False)
                mm(cum[:, 0, 1, :], tri_b, lf[:, 0, 1, :], start=False, stop=True).then_inc(cum_ready, 1)

                step(1)
                r = small[:, 1, :].rearrange("p (t d h) -> p t d h", t=2, d=2)

                def rows_of(h):
                    pe.wait_ge(gate_v, 3)
                    if h >= 2:
                        pe.wait_ge(ml_free, h - 1)
                    for d in range(2):
                        for t in range(NT):
                            c = (2 * d + t) * P
                            last = mm(psum[:, 6 + h % 2, c:c + P],
                                      r[:, t, d, h:h + 1].to_broadcast([P, P]), ident,
                                      start=True, stop=True)
                    last.then_inc(row_ready, 1)

                def qk(h):
                    pe.wait_ge(proj_saved, 3)
                    pe.wait_ge(ml_free, 4 + h - 1)
                    for t in range(NT):
                        last = mm(psum[:, 6 + h % 2, t * S:(t + 1) * S], qT[:, h, t * P:(t + 1) * P],
                                  kT[:, h, :], start=True, stop=True)
                    last.then_inc(ml_s_ready, 1)

                def weights_T(h):
                    m = m0 + h
                    pe.wait_ge(ml_p_ready, h + 1)
                    wait_batch_bank(pe, m)
                    transposes(m, [score[:, h, 1 - t, t, sh * P:(sh + 1) * P]
                                   for sh in range(2) for t in range(NT)])

                def pv(h):
                    pe.wait_ge(pt_saved, h + 1)
                    pe.wait_ge(ml_free, 8)
                    if h >= 2:
                        pe.wait_ge(ml_h_saved, h - 1)
                    for t in range(NT):
                        for sh in range(2):
                            last = mm(psum[:, 6 + h % 2, t * P:(t + 1) * P],
                                      pT[:, h % 2, sh, t * P:(t + 1) * P],
                                      v_ml[:, sh, h * ML_D:(h + 1) * ML_D], start=sh == 0, stop=sh == 1)
                    last.then_inc(ml_h_ready, 1)

                rows_of(0)
                rows_of(1)
                step(2)
                rows_of(2)
                rows_of(3)
                step(3)
                qk(0)
                qk(1)
                step(4)
                qk(2)
                qk(3)
                step(5)
                step(6)
                weights_T(0)
                weights_T(1)
                pv(0)
                weights_T(2)
                pv(1)
                weights_T(3)
                pv(2)
                pv(3)

                s_bank = 2 * ((n0 + 6) % 2)
                m_na = m0 + ML_H + 2

                def na_scores(h):
                    blk, po = h // 2, 64 * (h % 2)
                    if h == 0:
                        pe.wait_ge(proj_saved, 7)
                    if h >= 2:
                        pe.wait_ge(na_max, h - 1)
                    for t in range(NT):
                        last = mm(psum[:, s_bank + h % 2, t * S:(t + 1) * S],
                                  qT[po:po + 64, blk, t * P:(t + 1) * P], kT[po:po + 64, blk, :],
                                  start=True, stop=True)
                    last.then_inc(na_s_ready, 1)

                def na_transposes(h):
                    m = m_na + h
                    pe.wait_ge(na_p, h + 1)
                    wait_batch_bank(pe, m)
                    transposes(m, [na_s[:, h % 2, t * S + kh * P:t * S + (kh + 1) * P]
                                   for kh in range(2) for t in range(NT)])

                def na_pv(h):
                    blk, po = h // 2, 64 * (h % 2)
                    pe.wait_ge(pt_saved, ML_H + h + 1)
                    if h < 4:
                        pe.wait_ge(ml_h_saved, ML_H)
                    elif h % 2 == 0:
                        pe.wait_ge(ya_lo, blk - 1)
                    for kh in range(2):
                        last = mm(psum[po:po + 64, 6 + blk % 2, 0:S], v_na[:, kh, h * NA_D:(h + 1) * NA_D],
                                  pT[:, h % 2, kh, :], start=kh == 0, stop=kh == 1)
                    last.then_inc(na_o_ready, 1)

                na_scores(0)
                na_scores(1)
                pe.wait_ge(yb_ready, 1)
                for i in range(2):
                    m = m0 + ML_H + i
                    wait_batch_bank(pe, m)
                    transposes(m, [h_ml[:, t, (2 * i + hh) * P:(2 * i + hh + 1) * P]
                                   for hh in range(2) for t in range(NT)])
                for h in range(NA_H + 1):
                    if h < NA_H:
                        na_transposes(h)
                    if h + 2 < NA_H:
                        na_scores(h + 2)
                    if h >= 1:
                        na_pv(h - 1)

                def wait_blocks(j):
                    if j == 0:
                        pe.wait_ge(ya_lo, 4)
                    if j == 2:
                        pe.wait_ge(tp_lo, kind_count(m0 + ML_H + 1))

                output(phase, lambda kb: (yaT_hi if kb < 4 else ybT_hi)[:, kb % 4, :],
                       lambda kb: (yaT_lo if kb < 4 else ybT_lo)[:, kb % 4, :],
                       lambda: pe.wait_ge(proj_saved, 6), wait_blocks)

            def conv(phase):
                g0, n0 = GROUP0[phase], STEP0[phase]
                x_half(phase, 0)
                x_half(phase, 1)
                for i in range(PHASES[phase][1]):
                    if i >= 2:
                        pe.wait_ge(conv_read, i - 1)
                    slots = [(g0 + 2 * i) % RING, (g0 + 2 * i + 1) % RING]
                    transposed_step((n0 + i) % 2, slots, g0 + 2 * i).then_inc(proj_ready, 1)
                output(phase, lambda kb: zT_hi[:, kb, :], lambda kb: zT_lo[:, kb, :],
                       lambda: pe.wait_ge(conv_read, PHASES[phase][1] - 1),
                       lambda j: pe.wait_ge(z_lo, j // 2 + 1))

            for phase, (kind, _, _) in enumerate(PHASES):
                {FFN: ffn, MIX: mix, CONV: conv}[kind](phase)

        @block.scalar
        def _(act):
            copy = nc.scalar.copy

            counts = {"group": group_used, "proj": proj_ready, "acc": acc_ready}

            def split_hi(g, later=0):
                if g >= GROUPS:
                    return
                slot = g % RING
                act.wait_ge(raw_in[slot], later * FILL + (g // RING + 1) * FILL)
                if g >= RING:
                    which, value = USED[g - RING]
                    act.wait_ge(counts[which], later * {"group": 2, "proj": 4, "acc": 0}[which] + value)
                copy(w_hi[:, slot, :], raw[:, slot, :]).then_inc(hi_made, 1)

            def batch_hi(m, dst, view):
                act.wait_ge(tp_ready, m + 1)
                copy(dst, view(batch_bank(m))).then_inc(tp_hi, 1)

            def x_in_phase(phase):
                m = x_batch(phase)
                for t in range(NT):
                    for c in range(2):
                        batch_hi(m, xT_hi[:, 4 * c:4 * c + 4, t * P:(t + 1) * P],
                                 lambda b: b.rearrange("p (k n) -> p k n", k=4))
                        m += 1
                    if t == 0:
                        if phase == 0:
                            split_hi(0)
                            split_hi(1)
                        else:
                            split_hi(GROUP0[phase] - 1 + LEAD)
                if phase == 0:
                    split_hi(2)
                nc.scalar.mul(ax[:, :, :], xs[:, :, :], ALPHA).then_inc(ax_ready, 1)

            def ffn(phase):
                g0, n0, m0 = GROUP0[phase], STEP0[phase], BATCH0[phase]
                h0 = sum(k == FFN for k, _, _ in PHASES[:phase]) * FSTEPS
                lo0 = kind_count(m0) - 1

                def evacuate(s, off):
                    par = (n0 + off) % 2
                    act.wait_ge(proj_ready, s * 2 + (2 * (n0 + off) + 2))
                    act.wait_ge(tp_ready, s + (m0 + off - 1))
                    nc.scalar.activation(hid[:, off % 2, :, :], pair(par)[:, :, 0:256],
                                         ACT.Silu).then_inc(silu_ready, 1)

                def hid_hi(s, off):
                    act.wait_ge(tp_ready, s + (m0 + off + 1))
                    copy(hT_hi[:, bass.ds(s * 2 + 2 * off, 2), :],
                         psum[:, 4 + (m0 + off) % 2, :].rearrange("p (k n) -> p k n", k=2)
                         ).then_inc(tp_hi, 1)

                x_in_phase(phase)
                split_hi(g0 + LEAD)
                split_hi(g0 + 1 + LEAD)
                if phase == 0:
                    act.wait_ge(wg_in, 32)
                    copy(wg_hi[:, :, :], wg[:, :, :]).then_inc(wg_split, 1)
                for off in (1, 2):
                    evacuate(0, off - 1)
                    split_hi(g0 + 2 * off + LEAD)
                    hid_hi(0, off - 1)
                    split_hi(g0 + 2 * off + 1 + LEAD)
                with act.Fori(1, (FSTEPS - 1) // 2) as it:
                    for off in (0, 1):
                        evacuate(it * 2, off)
                        g = g0 + 4 + 2 * (off + 1) + LEAD
                        split_hi(g, it - 1)
                        hid_hi(it * 2, off)
                        split_hi(g + 1, it - 1)
                g1 = g0 + 2 * FSTEPS
                evacuate(FSTEPS - 1, 0)
                split_hi(g1 + LEAD)
                hid_hi(FSTEPS - 1, 0)
                for j in range(1, FKB // 2 - 1):
                    split_hi(g1 + j + LEAD)

            def mix(phase):
                g0, n0, m0 = GROUP0[phase], STEP0[phase], BATCH0[phase]
                dest = {"vb": v_ml, "ob": o_gate, "va": v_na, "qb": qT, "kb": kT, "qa": qT, "ka": kT}

                def evacuate(i):
                    name = MIX_COLS[i]
                    act.wait_ge(proj_ready, 2 * (n0 + i) + 2)
                    if name == "qa":
                        act.wait_ge(ml_s_ready, ML_H)
                    src = pair((n0 + i) % 2)
                    dst = dest[name][:, :, :]
                    if name in TRANSPOSED:
                        src = src.rearrange("p b (c n) -> p (b c) n", c=2)
                    if name == "ob":
                        ins = nc.scalar.activation(dst, src, ACT.Sigmoid)
                    elif name == "qa":
                        ins = nc.scalar.mul(dst, src, float(NA_D) ** -0.5)
                    elif name == "kb":
                        ins = nc.scalar.mul(dst, src, float(ML_D) ** -0.5)
                    else:
                        ins = copy(dst, src)
                    ins.then_inc(proj_saved, 1)

                x_in_phase(phase)
                split_hi(g0 + LEAD)
                act.wait_ge(gate_v, 1)
                nc.scalar.activation(small[:, 3, :], small[:, 2, :], ACT.Exp).then_inc(gate_a, 1)
                act.wait_ge(gate_a, 1)
                nc.scalar.activation(small[:, 4, :], small[:, 3, :], ACT.Ln, bias=1.0).then_inc(gate_a, 1)
                split_hi(g0 + 1 + LEAD)

                def ml_exp(h):
                    act.wait_ge(max_ready, 1)
                    for d in range(2):
                        for t in range(NT):
                            lo, hi = allowed(d, t)
                            k = (t * 2 + d) * ML_H + h
                            v = score[:, h, d, t, lo:hi]
                            last = nc.scalar.activation(v, v, ACT.Exp, bias=small[:, 6, k:k + 1])
                    last.then_inc(ml_w_ready, 1)

                for i in range(1, 7):
                    evacuate(i - 1)
                    split_hi(g0 + 2 * i + LEAD)
                    if i == 4:
                        ml_exp(0)
                        ml_exp(1)
                    if i == 5:
                        ml_exp(2)
                        ml_exp(3)
                        act.wait_ge(gate_v, 4)
                        nc.scalar.activation(small[:, 8, :], small[:, 7, :], ACT.Exp,
                                             scale=-1.0).then_inc(gate_a, 1)
                    split_hi(g0 + 2 * i + 1 + LEAD)
                evacuate(6)

                def save_pT(m, i):
                    act.wait_ge(tp_ready, m + 1)
                    copy(pT[:, i % 2, :, :], batch_bank(m).rearrange("p (a n) -> p a n", a=2)
                         ).then_inc(pt_saved, 1)

                def save_h(h):
                    act.wait_ge(ml_h_ready, h + 1)
                    copy(h_ml[:, :, h * P:(h + 1) * P],
                         psum[:, 6 + h % 2, 0:S].rearrange("p (t n) -> p t n", t=2)
                         ).then_inc(ml_h_saved, 1)

                for h in range(ML_H):
                    if h >= 2:
                        act.wait_ge(ml_h_ready, h - 1)
                    save_pT(m0 + h, h)
                    if h >= 1:
                        save_h(h - 1)
                save_h(ML_H - 1)

                m_na = m0 + ML_H + 2

                def na_exp_of(h):
                    act.wait_ge(na_max, h + 1)
                    for t in range(NT):
                        v = na_s[:, h % 2, t * S:(t + 1) * S]
                        c = 2 * h + t
                        last = nc.scalar.activation(v, v, ACT.Exp, bias=small[:, 10, c:c + 1],
                                                    accum_out=small[:, 11, c:c + 1])
                    last.then_inc(na_exp, 1)

                def na_save_pT(h):
                    if h >= 2:
                        act.wait_ge(na_o_ready, h - 1)
                    save_pT(m_na + h, h)

                def out_hi(blk):
                    act.wait_ge(na_o_ready, 2 * blk + 2)
                    copy(yaT_hi[:, blk, :], psum[:, 6 + blk % 2, 0:S]).then_inc(ya_hi, 1)

                def ybT(i):
                    batch_hi(m0 + ML_H + i, ybT_hi[:, 2 * i:2 * i + 2, :],
                             lambda b: b.rearrange("p (k n) -> p k n", k=2))

                na_exp_of(0)
                ybT(0)
                ybT(1)
                for i in range(1, NA_H + 3):
                    if i < NA_H:
                        na_exp_of(i)
                    if i <= NA_H:
                        na_save_pT(i - 1)
                    if i >= 4 and i % 2 == 0:
                        out_hi((i - 4) // 2)
                g1 = g0 + 14
                for j in range(KB // 2 - 1):
                    split_hi(g1 + j + LEAD)

            def conv(phase):
                g0, n0 = GROUP0[phase], STEP0[phase]
                x_in_phase(phase)
                n_steps = PHASES[phase][1]
                for i in range(n_steps + 1):
                    if i < n_steps:
                        split_hi(g0 + 2 * i + LEAD)
                        split_hi(g0 + 2 * i + 1 + LEAD)
                    if i in (3, 6):
                        j = i // 3 - 1
                        act.wait_ge(conv_read, i)
                        copy(zT_hi[:, 4 * j:4 * j + 4, :], zT[:, :, :]).then_inc(z_hi, 1)
                for j in range(KB // 2 - 1):
                    split_hi(g0 + 2 * n_steps + j + LEAD)

            for phase, (kind, _, _) in enumerate(PHASES):
                {FFN: ffn, MIX: mix, CONV: conv}[kind](phase)

        @block.vector
        def _(dve):
            vec = nc.vector
            steps = 0

            def wait_step_result():
                dve.wait_ge(v_step, steps)

            def counted(ins):
                nonlocal steps
                steps += 1
                ins.then_inc(v_step, 1)

            def split_lo(g, slot=None):
                if isinstance(g, int):
                    if g >= GROUPS:
                        return
                    slot = g % RING
                dve.wait_ge(hi_made, g + 1)
                vec.tensor_tensor(w_lo[:, slot, :], raw[:, slot, :], w_hi[:, slot, :].bitcast(F32),
                                  ALU.subtract).then_inc(lo_made, 1)

            def batch_lo(m, hi, dst, view):
                dve.wait_ge(tp_hi, kind_count(m))
                vec.tensor_tensor(dst, view(batch_bank(m)), hi.bitcast(F32), ALU.subtract).then_inc(tp_lo, 1)

            def x_lo(phase, t):
                for c in range(2):
                    a = (slice(None), slice(4 * c, 4 * c + 4), slice(t * P, (t + 1) * P))
                    batch_lo(x_batch(phase) + 2 * t + c, xT_hi[a], xT_lo[a],
                             lambda b: b.rearrange("p (k n) -> p k n", k=4))

            rstds = 0

            def norm(phase, scale):
                banks = [pair(acc_pair(phase)), psum[:, 6:8, :]]
                dve.wait_ge(gb_in, 32 * (phase + 1))
                dve.wait_ge(ax_ready, phase + 1)

                def sums(t):
                    dve.wait_ge(acc_ready, 2 * phase + t + 1)
                    for c in range(2):
                        cs = slice(c * 512, (c + 1) * 512)
                        counted(vec.scalar_tensor_tensor(out=xs[:, t, cs], in0=banks[t][:, c, :], scalar=scale,
                                                         in1=ax[:, t, cs], op0=ALU.mult, op1=ALU.add))
                    return steps

                def moments(t, summed):
                    for c in range(2):
                        dve.wait_ge(v_step, summed - 1 + c)
                        counted(vec.bn_stats(stats[:, c, :], xs[:, t, c * 512:(c + 1) * 512]))
                    wait_step_result()
                    counted(vec.bn_aggr(mv[:, t, :], stats[:, :, :]))
                    wait_step_result()
                    vec.tensor_scalar(var_eps[:, 0:1], mv[:, t, 1:2], EPS, None, ALU.add).then_inc(var_ready, 1)

                def scaled(t):
                    nonlocal rstds
                    rstds += 1
                    for c in range(2):
                        cs = slice(c * 512, (c + 1) * 512)
                        counted(vec.scalar_tensor_tensor(out=xs[:, t, cs], in0=xs[:, t, cs],
                                                         scalar=mv[:, t, 0:1], in1=gb[:, 0, cs],
                                                         op0=ALU.subtract, op1=ALU.mult))
                    dve.wait_ge(rstd_ready, rstds)
                    for c in range(2):
                        cs = slice(c * 512, (c + 1) * 512)
                        dve.wait_ge(v_step, steps - 1 + c)
                        vec.scalar_tensor_tensor(out=xs[:, t, cs], in0=xs[:, t, cs], scalar=rstd[:, 0:1],
                                                 in1=gb[:, 1, cs], op0=ALU.mult,
                                                 op1=ALU.add).then_inc(x_ready, 1)

                moments(0, sums(0))
                scaled(0)
                summed = sums(1)
                if phase < LAST:
                    x_lo(phase + 1, 0)
                moments(1, summed)
                scaled(1)
                if phase < LAST:
                    x_lo(phase + 1, 1)
                    split_lo(GROUP0[phase + 1] - 1 + LEAD)

            def ffn(phase):
                g0, n0, m0 = GROUP0[phase], STEP0[phase], BATCH0[phase]
                h0 = sum(k == FFN for k, _, _ in PHASES[:phase]) * FSTEPS
                lo0 = kind_count(m0) - 1

                def hidden(s, off):
                    par = (n0 + off) % 2
                    dve.wait_ge(silu_ready, s + (h0 + off + 1))
                    vec.tensor_tensor(hid[:, off % 2, :, :], hid[:, off % 2, :, :], pair(par)[:, :, 256:512],
                                      ALU.mult).then_inc(hid_ready, 1)

                def hid_lo(s, off):
                    dve.wait_ge(tp_hi, s + (lo0 + off + 1))
                    dst = bass.ds(s * 2 + 2 * off, 2)
                    vec.tensor_tensor(hT_lo[:, dst, :],
                                      psum[:, 4 + (m0 + off) % 2, :].rearrange("p (k n) -> p k n", k=2),
                                      hT_hi[:, dst, :].bitcast(F32), ALU.subtract).then_inc(tp_lo, 1)

                split_lo(g0 + LEAD)
                split_lo(g0 + 1 + LEAD)
                if phase == 0:
                    dve.wait_ge(wg_split, 1)
                    vec.tensor_tensor(wg_lo[:, :, :], wg[:, :, :], wg_hi[:, :, :].bitcast(F32),
                                      ALU.subtract).then_inc(wg_split, 1)
                for off in (1, 2):
                    hidden(0, off - 1)
                    split_lo(g0 + 2 * off + LEAD)
                    hid_lo(0, off - 1)
                    split_lo(g0 + 2 * off + 1 + LEAD)
                with dve.Fori(1, (FSTEPS - 1) // 2) as it:
                    for off in (0, 1):
                        hidden(it * 2, off)
                        g = g0 + 2 * (off + 1) + LEAD
                        split_lo(it * 4 + g, g % RING)
                        hid_lo(it * 2, off)
                        split_lo(it * 4 + (g + 1), (g + 1) % RING)
                g1 = g0 + 2 * FSTEPS
                hidden(FSTEPS - 1, 0)
                split_lo(g1 + LEAD)
                hid_lo(FSTEPS - 1, 0)
                for j in range(1, FKB // 2 - 1):
                    split_lo(g1 + j + LEAD)
                norm(phase, 0.5)

            def mix(phase):
                nonlocal rstds
                dve.wait_ge(cst_in, 16)
                g0, n0, m0 = GROUP0[phase], STEP0[phase], BATCH0[phase]
                pre = small[:, 12:14, :]
                by = pre.rearrange("p t (d k h) -> p t d k h", d=2, k=2)
                flat = lambda row: small[:, row, :].rearrange("p (t d h) -> p t d h", t=2, d=2)

                dve.wait_ge(gates_ready, 1)
                for t in range(NT):
                    counted(vec.tensor_tensor(pre[:, t, :], psum[:, 4, t * N_GATES:(t + 1) * N_GATES],
                                              gate_bias[:, :], ALU.add))
                wait_step_result()
                for t in range(NT):
                    f = by[:, t, :, 1, :]
                    last = vec.scalar_tensor_tensor(out=flat(2)[:, t], in0=f, scalar=-1.0, in1=f,
                                                    op0=ALU.mult, op1=ALU.min)
                last.then_inc(gate_v, 1)
                split_lo(g0 + LEAD)
                dve.wait_ge(gate_a, 2)
                for t in range(NT):
                    last = vec.scalar_tensor_tensor(out=flat(0)[:, t], in0=by[:, t, :, 1, :], scalar=0.0,
                                                    in1=flat(4)[:, t], op0=ALU.min, op1=ALU.subtract)
                last.then_inc(gate_v, 1)
                split_lo(g0 + 1 + LEAD)

                dve.wait_ge(cum_ready, 1)
                counted(vec.tensor_copy(small[:, 5, :], psum[:, 5, 0:16]))
                wait_step_result()
                for t in range(NT):
                    last = vec.tensor_tensor(flat(1)[:, t], by[:, t, :, 0, :], flat(5)[:, t], ALU.subtract)
                last.then_inc(gate_v, 1)

                def split2(i):
                    split_lo(g0 + 2 * i + LEAD)
                    split_lo(g0 + 2 * i + 1 + LEAD)

                def maxima(h):
                    dve.wait_ge(row_ready, h + 1)
                    for d in range(2):
                        for t in range(NT):
                            lo, hi = allowed(d, t)
                            k = (t * 2 + d) * ML_H + h
                            mask = (mask_f if d == 0 else mask_b)
                            m_lo = mask_start(d, t)
                            last = vec.tensor_tensor_reduce(
                                score[:, h, d, t, lo:hi], psum[:, 6 + h % 2, d * S + lo:d * S + hi],
                                mask[:, m_lo:m_lo + hi - lo], 1.0, 0.0, ALU.add, ALU.max,
                                small[:, 14, k:k + 1])
                    last.then_inc(ml_free, 1)

                def weigh(h):
                    dve.wait_ge(ml_s_ready, h + 1)
                    dve.wait_ge(ml_w_ready, h + 1)
                    for d in range(2):
                        for t in range(NT):
                            lo, hi = allowed(d, t)
                            k = (t * 2 + d) * ML_H + h
                            v = score[:, h, d, t, lo:hi]
                            last = vec.tensor_tensor_reduce(
                                v, v, psum[:, 6 + h % 2, t * S + lo:t * S + hi], 1.0, 0.0,
                                ALU.mult, ALU.add, small[:, 15, k:k + 1])
                    last.then_inc(ml_free, 1)

                def combine(h):
                    for t in range(NT):
                        full, part = 1 - t, t
                        lo, hi = t * P, (t + 1) * P
                        kf = (t * 2 + full) * ML_H + h
                        kp = (t * 2 + part) * ML_H + h
                        whole = score[:, h, full, t, :]
                        counted(vec.tensor_scalar(whole, whole, small[:, 9, kf:kf + 1], None, ALU.mult))
                        wait_step_result()
                        last = vec.scalar_tensor_tensor(
                            out=score[:, h, full, t, lo:hi], in0=score[:, h, part, t, lo:hi],
                            scalar=small[:, 9, kp:kp + 1], in1=score[:, h, full, t, lo:hi],
                            op0=ALU.mult, op1=ALU.add)
                    last.then_inc(ml_p_ready, 1)

                split2(1)
                maxima(0)
                split_lo(g0 + 4 + LEAD)
                maxima(1)
                split_lo(g0 + 5 + LEAD)
                maxima(2)
                split_lo(g0 + 6 + LEAD)
                maxima(3)
                dve.wait_ge(ml_free, 4)
                vec.tensor_tensor(small[:, 7, :], small[:, 5, :], small[:, 14, :],
                                  ALU.add).then_inc(gate_v, 1)
                vec.tensor_scalar(small[:, 6, :], small[:, 14, :], -1.0, None, ALU.mult).then_inc(max_ready, 1)
                split_lo(g0 + 7 + LEAD)
                weigh(0)
                split_lo(g0 + 8 + LEAD)
                weigh(1)
                split_lo(g0 + 9 + LEAD)
                weigh(2)
                split_lo(g0 + 10 + LEAD)
                weigh(3)
                dve.wait_ge(ml_free, 8)
                counted(vec.scalar_tensor_tensor(out=small[:, 3, :], in0=small[:, 15, :], scalar=-1.0,
                                                 in1=small[:, 15, :], op0=ALU.mult, op1=ALU.max))
                dve.wait_ge(gate_a, 3)
                wait_step_result()
                counted(vec.tensor_tensor(small[:, 4, :], small[:, 3, :], small[:, 8, :], ALU.max))
                wait_step_result()
                counted(vec.reciprocal(small[:, 9, :], small[:, 4, :]))
                split_lo(g0 + 11 + LEAD)
                wait_step_result()
                combine(0)
                combine(1)
                split_lo(g0 + 12 + LEAD)
                combine(2)
                combine(3)
                split_lo(g0 + 13 + LEAD)

                def rpb_keys(h, j):
                    v = rpb[:, h, j:j + ROWS, :]
                    (pitch, n), (row, _), (one, _) = v.ap
                    return bass.AP(v.tensor, v.offset + GRID_W - 1, [[pitch, n], [row, ROWS], [-one, GRID_W]])

                def na_maxima(h):
                    if h == 0:
                        dve.wait_ge(rpb_made, 1)
                    dve.wait_ge(na_s_ready, h + 1)
                    if h >= 2:
                        dve.wait_ge(tp_ready, m_na + h - 1)
                    for t in range(NT):
                        j = 2 - 2 * t
                        c = 2 * h + t
                        counted(vec.tensor_tensor_reduce(
                            na_s[:, h % 2, t * S:(t + 1) * S].rearrange("p (j c) -> p j c", j=ROWS),
                            psum[:, s_bank + h % 2, t * S:(t + 1) * S].rearrange("p (j c) -> p j c", j=ROWS),
                            rpb_keys(h, j),
                            1.0, -3e38, ALU.add, ALU.max, small[:, 12, c:c + 1]))
                    wait_step_result()
                    vec.tensor_scalar(small[:, 10, 2 * h:2 * h + 2], small[:, 12, 2 * h:2 * h + 2], -1.0, None,
                                      ALU.mult).then_inc(na_max, 1)

                def na_norm(h):
                    dve.wait_ge(na_exp, h + 1)
                    counted(vec.reciprocal(small[:, 13, 2 * h:2 * h + 2], small[:, 11, 2 * h:2 * h + 2]))
                    wait_step_result()
                    for t in range(NT):
                        v = na_s[:, h % 2, t * S:(t + 1) * S]
                        c = 2 * h + t
                        last = vec.tensor_scalar(v, v, small[:, 13, c:c + 1], None, ALU.mult)
                    last.then_inc(na_p, 1)

                def out_lo(blk):
                    dve.wait_ge(ya_hi, blk + 1)
                    vec.tensor_tensor(yaT_lo[:, blk, :], psum[:, 6 + blk % 2, 0:S],
                                      yaT_hi[:, blk, :].bitcast(F32), ALU.subtract).then_inc(ya_lo, 1)

                s_bank = 2 * ((n0 + 6) % 2)
                m_na = m0 + ML_H + 2

                st = score[:, 0, 0, 0, 0:48].rearrange("p (a b) -> p a b", a=8)
                agg = score[:, 0, 0, 0, 64:80].rearrange("p (a b) -> p a b", a=8)
                dve.wait_ge(gn_in, 16)
                for t in range(NT):
                    counted(vec.tensor_tensor(o_gate[:, t, :], o_gate[:, t, :], gn_gain[:, :], ALU.mult))
                dve.wait_ge(ml_h_saved, ML_H)
                for t in range(NT):
                    for h in range(ML_H):
                        counted(vec.bn_stats(st[:, t * 4 + h, :], h_ml[:, t, h * P:(h + 1) * P]))
                wait_step_result()
                for i in range(8):
                    counted(vec.bn_aggr(agg[:, i, :], st[:, i, :]))
                wait_step_result()
                vec.tensor_scalar(var_eps[:, 0:8], agg[:, :, 1], EPS, None, ALU.add).then_inc(var_ready, 1)
                rstds += 1
                dve.wait_ge(rstd_ready, rstds)
                for t in range(NT):
                    for h in range(ML_H):
                        i = t * 4 + h
                        v = h_ml[:, t, h * P:(h + 1) * P]
                        counted(vec.tensor_scalar(v, v, agg[:, i, 0:1], rstd[:, i:i + 1],
                                                  ALU.subtract, ALU.mult))
                wait_step_result()
                vec.tensor_tensor(h_ml, h_ml, o_gate[:, :, :], ALU.mult).then_inc(yb_ready, 1)
                na_maxima(0)
                for i in range(2):
                    a = ybT_hi[:, 2 * i:2 * i + 2, :]
                    batch_lo(m0 + ML_H + i, a, ybT_lo[:, 2 * i:2 * i + 2, :],
                             lambda b: b.rearrange("p (k n) -> p k n", k=2))
                for i in range(1, NA_H + 3):
                    if i < NA_H:
                        na_maxima(i)
                    if i <= NA_H:
                        na_norm(i - 1)
                    if i >= 4 and i % 2 == 0:
                        out_lo((i - 4) // 2)
                for j in range(KB // 2 - 1):
                    split_lo(g0 + 14 + j + LEAD)
                norm(phase, 1.0)

            def conv(phase):
                g0, n0 = GROUP0[phase], STEP0[phase]
                counted(vec.memset(uT[:, :, 0:1], 0.0))
                counted(vec.memset(uT[:, :, S + 1:S + 2], 0.0))
                split_lo(g0 + LEAD)
                split_lo(g0 + 1 + LEAD)
                dve.wait_ge(taps_in, 16)
                n_steps = PHASES[phase][1]
                for i in range(n_steps):
                    part, j = CONV_STEPS[i]
                    src = pair((n0 + i) % 2).rearrange("p b (c n) -> p (b c) n", c=2)
                    dve.wait_ge(proj_ready, 2 * (n0 + i) + 2)
                    if part == 1:
                        vec.tensor_copy(cgT[:, :, :], src).then_inc(conv_read, 1)
                    if part == 2:
                        dve.wait_ge(conv_read, i)
                        vec.tensor_tensor(uT[:, :, 1:S + 1], src, cgT[:, :, :], ALU.mult).then_inc(conv_read, 1)
                        dve.wait_ge(conv_read, i + 1)
                        wait_step_result()
                        for tap in (1, 0, 2):
                            for b in range(4):
                                w = taps[:, 4 * j + b, :]
                                u = uT[:, b, tap:tap + S]
                                if tap == 1:
                                    counted(vec.tensor_scalar(yT[:, b, :], u, w[:, 1:2], w[:, 3:4],
                                                              ALU.mult, ALU.add))
                                else:
                                    dve.wait_ge(v_step, steps - 3)
                                    counted(vec.scalar_tensor_tensor(out=yT[:, b, :], in0=u,
                                                                     scalar=w[:, tap:tap + 1], in1=yT[:, b, :],
                                                                     op0=ALU.mult, op1=ALU.add))
                    if part == 0:
                        wait_step_result()
                        if j == 1:
                            dve.wait_ge(z_hi, 1)
                        vec.tensor_tensor(zT[:, :, :], src, yT[:, :, :], ALU.mult).then_inc(conv_read, 1)
                    if i + 1 < n_steps:
                        split_lo(g0 + 2 * (i + 1) + LEAD)
                        split_lo(g0 + 2 * (i + 1) + 1 + LEAD)
                    if part == 0:
                        dve.wait_ge(z_hi, j + 1)
                        vec.tensor_tensor(zT_lo[:, 4 * j:4 * j + 4, :], zT[:, :, :],
                                          zT_hi[:, 4 * j:4 * j + 4, :].bitcast(F32),
                                          ALU.subtract).then_inc(z_lo, 1)
                for j in range(KB // 2 - 1):
                    split_lo(g0 + 2 * n_steps + j + LEAD)
                norm(phase, 1.0)

            x_lo(0, 0)
            split_lo(0)
            split_lo(1)
            x_lo(0, 1)
            split_lo(2)
            for phase, (kind, _, _) in enumerate(PHASES):
                {FFN: ffn, MIX: mix, CONV: conv}[kind](phase)


_INS = ["x", "ln_g", "ln_b", "ab_gate_b", "na_rpb", "ml_gn_g"]


def weight_groups(ffn_w_in, ffn_w_out, ab_w_in, ab_w_out, sc_w_in, sc_w_out):
    groups = np.empty((GROUPS, P, TILES * 512), np.float32)
    at = 0

    def put(a):
        nonlocal at
        n = a.shape[0]
        groups[at:at + n].reshape(a.shape)[...] = a
        at += n

    def columns(w, c0):
        put(w[:, c0:c0 + 512].reshape(2, 4, P, 512).transpose(0, 2, 1, 3))

    def rows(w):
        put(w.reshape(-1, 2, P, D).transpose(0, 2, 1, 3))

    for phase, (kind, _, _) in enumerate(PHASES):
        layer, i = divmod(phase, 3)
        if kind == FFN:
            w = ffn_w_in[layer, i // 2].reshape(2, 4, P, 2, FSTEPS, 256).transpose(4, 0, 2, 1, 3, 5)
            for step in w:
                put(step)
            rows(ffn_w_out[layer, i // 2])
        elif kind == MIX:
            for name in MIX_COLS:
                columns(ab_w_in[0], 512 * MIX_AT[name])
            rows(ab_w_out[0])
        else:
            for part, half in CONV_STEPS:
                columns(sc_w_in[0], part * D + half * 512)
            rows(sc_w_out[0])
    return groups.reshape(GROUPS * P, TILES * 512)


def kernel(**inputs):
    import concourse.bacc as bacc
    from concourse.bass_utils import run_bass_kernel_spmd

    nc = bacc.Bacc("TRN2", target_bir_lowering=False, num_devices=1)
    given = {n: np.asarray(a) for n, a in inputs.items()}
    laid_out = {n: given[n] for n in _INS}
    laid_out["na_rpb"] = given["na_rpb"][..., ::-1]
    laid_out["weights"] = weight_groups(*[given[n] for n in (
        "ffn_w_in", "ffn_w_out", "ab_w_in", "ab_w_out", "sc_w_in", "sc_w_out")])
    laid_out["gate_w"] = given["ab_w_in"][0, :, 7 * 512:].reshape(KB, P, N_GATES).transpose(1, 0, 2)
    laid_out["conv_taps"] = np.concatenate([given["sc_conv_w"][0], given["sc_conv_b"]]).reshape(
        4, KB, P).transpose(2, 1, 0)
    laid_out["consts"] = constants()
    arrays, args = {}, []
    for name, a in laid_out.items():
        a = np.ascontiguousarray(a)
        arrays[f"in_{name}"] = a
        args.append(nc.dram_tensor(f"in_{name}", a.shape, mybir.dt.from_np(a.dtype), kind="ExternalInput").ap())
    args.append(nc.dram_tensor("out_0", (1, S, D), F32, kind="ExternalOutput").ap())
    build(nc, *args)
    r = run_bass_kernel_spmd(nc, [arrays], core_ids=[0])
    return r.results[0]["out_0"]
```

```python
from contextlib import ExitStack

import numpy as np

import concourse.bass as bass
from concourse import mybir

ALU = mybir.AluOpType
ACT = mybir.ActivationFunctionType
F32 = mybir.dt.float32
F32R = mybir.dt.float32r

P = 128
D = 1024
S = 256
NT = S // P
KB = D // P
FF = 2816
FKB = FF // P
FSTEPS = FF // 256
HALF_D = D // 2
NA_H, NA_D = 8, 64
ML_H, ML_D = 4, 128
GRID_W, WIN_W = 64, 16
ROWS = S // GRID_W
RPB_R, RPB_C = 15, 31
N_GATES = 4 * ML_H
ALPHA = 4.0 ** 0.25
EPS = 1e-5
NEG = -1e30

RING = 4
TILES = 4
LEAD = 3
FILL = 16

FFN, MIX, CONV = "ffn", "mix", "conv"
MIX_COLS = ["va", "qa", "ka", "qb", "kb", "vb", "ob"]
MIX_AT = {n: i for i, n in enumerate(["qa", "ka", "va", "qb", "kb", "vb", "ob"])}
TRANSPOSED = ("qb", "kb", "qa", "ka")
PHASES = [(FFN, FSTEPS, FKB), (MIX, len(MIX_COLS), KB), (FFN, FSTEPS, FKB),
          (FFN, FSTEPS, FKB), (CONV, 3 * D // 512, KB), (FFN, FSTEPS, FKB)]
CONV_STEPS = [(1, 0), (2, 0), (0, 0), (1, 1), (2, 1), (0, 1)]

USED = []
GROUP0, STEP0, BATCH0 = [], [], []
_g = _n = 0
_m = 4
for _kind, _steps, _kb in PHASES:
    GROUP0.append(_g)
    STEP0.append(_n)
    BATCH0.append(_m)
    _g += 2 * _steps + _kb // 2
    _n += _steps
    for _i in range(_steps):
        USED += [("group", sum(u[0] == "group" for u in USED) + 1), ("proj", 2 * (STEP0[-1] + _i) + 2)]
    for _i in range(_kb // 2 - 1):
        USED.append(("group", sum(u[0] == "group" for u in USED) + 1))
    USED.append(("acc", 4 * len(GROUP0)))
    _m += (FSTEPS if _kind == FFN else 0) + 4
GROUPS = _g
LAST = len(PHASES) - 1


FIRST_TILES = [(g, i) for g in range(2) for i in range(TILES)]


def tile_cols(i):
    return slice(i * 512, (i + 1) * 512)


def x_batch(phase):
    return BATCH0[phase] - 4


def acc_pair(phase):
    return (STEP0[phase] + PHASES[phase][1] + (PHASES[phase][0] == MIX)) % 2


ROW_QUARTERS = [7, 8, 9, 11]
NA_QUARTER = 12
QK_QUARTERS = [22, 23, 24, 25]
ML_QUARTER = 27


def ml_bank(h):
    return 5 if h % 2 else 7


def splits_after(i, q):
    late = 3 if MIX_COLS[i] in TRANSPOSED else 2
    return [2 * i + LEAD] * (q == 0) + [2 * i + 1 + LEAD] * (q == late)


def constants():
    s = np.arange(P)[:, None]
    t = np.arange(P)[None, :]
    cols = [np.eye(P), s <= t, s >= t, np.ones((P, P)),
            np.zeros((P, P)), np.where(t <= s, 0, NEG),
            np.where(t >= s, 0, NEG), np.zeros((P, P))]
    c = np.arange(P)[:, None] % GRID_W
    kc = np.arange(GRID_W)[None, :]
    start = np.clip(c - WIN_W // 2, 0, GRID_W - WIN_W)
    cols.append(np.where((kc >= start) & (kc < start + WIN_W), 0, NEG)[:, ::-1])
    return np.concatenate([np.asarray(a, np.float32) for a in cols], axis=1)


def region(d, t):
    return (t * S, (t + 1) * S) if t != d else (2 * S + t * P, 2 * S + (t + 1) * P)


def allowed(d, t):
    return (0, S) if t != d else (t * P, (t + 1) * P)


def mask_start(d, t):
    return P if (d, t) == (0, 0) else 0


CONST_W = 8 * P + GRID_W


def build(nc, x, ln_g, ln_b, ab_gate_b, na_rpb, ml_gn_g, weights, gate_w, conv_taps, consts, out):
    ctx = ExitStack()
    with ctx:
        def sem(name):
            return ctx.enter_context(nc.semaphore(name))

        def sb(name, shape, dt=F32):
            return ctx.enter_context(nc.sbuf_tensor(name, shape, dt))

        raw = sb("raw", [P, RING, TILES * 512])
        w_hi = sb("w_hi", [P, RING, TILES * 512], F32R)
        w_lo = sb("w_lo", [P, RING, TILES * 512], F32R)
        xs = sb("xs", [P, NT, D])
        ax = sb("ax", [P, NT, D])
        xT_hi = sb("xT_hi", [P, KB, S], F32R)
        xT_lo = sb("xT_lo", [P, KB, S], F32R)
        gb = sb("gb", [P, 2, D])
        cst = sb("cst", [P, CONST_W])
        wg = sb("wg", [P, KB, N_GATES])
        wg_hi = sb("wg_hi", [P, KB, N_GATES], F32R)
        wg_lo = sb("wg_lo", [P, KB, N_GATES], F32R)
        gate_bias = sb("gate_bias", [N_GATES, 1])
        stats = sb("stats", [P, 2, 6])
        mv = sb("mv", [P, NT, 2])
        var_eps = sb("var_eps", [P, 8])
        rstd = sb("rstd", [P, 8])
        minus_half = sb("minus_half", [P, 8])
        small = sb("small", [P, 16, 16])
        ident = cst[:, 0:P]
        tri_f = cst[:, P:2 * P]
        tri_b = cst[:, 2 * P:3 * P]
        ones = cst[:, 3 * P:4 * P]
        mask_f = cst[:, 4 * P:6 * P]
        mask_b = cst[:, 6 * P:8 * P]
        mask_na = cst[:, 8 * P:8 * P + GRID_W]

        ARENA = 65792
        arena_at = -(-nc.sbuf_base // 32) * 32
        sb("arena", [P, ARENA // 4])
        at = {}

        def place(phase, name, shape, dt=F32):
            size = int(np.prod(shape[1:])) * 4
            offset = at.get(phase, 0)
            at[phase] = offset + size
            assert at[phase] <= ARENA, (phase, name, at[phase])
            return nc.alloc_sbuf_tensor_at(name, shape, dt, offset=arena_at + offset)

        hT_hi = place(FFN, "hT_hi", [P, FKB, S], F32R)
        hT_lo = place(FFN, "hT_lo", [P, FKB, S], F32R)
        hid = place(FFN, "hid", [P, 2, NT, 256])

        score = place(MIX, "score", [P, ML_H, 3 * S])
        yaT_hi = place(MIX, "yaT_hi", [P, 4, S], F32R)
        yaT_lo = place(MIX, "yaT_lo", [P, 4, S], F32R)
        q_ml = place(MIX, "q_ml", [P, 4, S])
        k_ml = place(MIX, "k_ml", [P, 4, S])
        ybT_hi = nc.alloc_sbuf_tensor_at("ybT_hi", [P, 4, S], F32R, offset=arena_at + at[MIX] - 8192)
        ybT_lo = nc.alloc_sbuf_tensor_at("ybT_lo", [P, 4, S], F32R, offset=arena_at + at[MIX] - 4096)
        q_na, k_na = (gb[:, j, :].rearrange("p (b n) -> p b n", b=4) for j in range(2))
        v_ml = place(MIX, "v_ml", [P, NT, 512])
        o_gate = place(MIX, "o_gate", [P, NT, 512])
        v_na = place(MIX, "v_na", [P, NT, 512])
        p_na = place(MIX, "p_na", [P, 2, NT, S])
        p_ml = place(MIX, "p_ml", [P, 2, NT, S])
        gates_T = nc.alloc_sbuf_tensor_at("gates_T", [N_GATES, S], F32,
                                          offset=arena_at + at[MIX] - 4096)
        rpb = place(MIX, "rpb", [P, NA_H, 6, GRID_W])
        gn_gain = place(MIX, "gn_gain", [P, 512])
        norm_stats = place(MIX, "norm_stats", [P, 8, 8])
        h_ml = xs[:, :, 0:512]
        na_s = xs[:, :, 512:1024]

        cgT = place(CONV, "cgT", [P, 4, S])
        uT = place(CONV, "uT", [P, 4, S + 2])
        yT = place(CONV, "yT", [P, 4, S])
        zT = place(CONV, "zT", [P, 4, S])
        zT_hi = place(CONV, "zT_hi", [P, KB, S], F32R)
        zT_lo = place(CONV, "zT_lo", [P, KB, S], F32R)
        taps = sb("taps", [P, KB, 4])

        psum = ctx.enter_context(nc.psum_tensor("psum", [P, 8, 512], F32))

        def pair(p):
            return psum[:, 2 * p:2 * p + 2, :]

        raw_in = [sem(f"raw_in{i}") for i in range(RING)]
        hi_made = sem("hi_made")
        lo_made = sem("lo_made")
        group_used = sem("group_used")
        proj_ready = sem("proj_ready")
        proj_saved = sem("proj_saved")
        conv_read = sem("conv_read")
        silu_ready = sem("silu_ready")
        hid_ready = sem("hid_ready")
        tp_ready = sem("tp_ready")
        tp_hi = sem("tp_hi")
        tp_lo = sem("tp_lo")
        acc_ready = sem("acc_ready")
        x_ready = sem("x_ready")
        ax_ready = sem("ax_ready")
        var_ready = sem("var_ready")
        rstd_ready = sem("rstd_ready")
        v_step = sem("v_step")
        p_step = sem("p_step")
        x_in = [sem(f"x_in{i}") for i in range(2 * NT)]
        tile_in = [sem(f"tile_in{i}") for i in range(2 * TILES - 1)]
        tile_hi = sem("tile_hi")
        tile_lo = sem("tile_lo")
        ident_in = sem("ident_in")
        cst_in = sem("cst_in")
        gb_in = sem("gb_in")
        wg_in = sem("wg_in")
        wg_split = sem("wg_split")
        rpb_in = sem("rpb_in")
        rpb_made = sem("rpb_made")
        gates_ready = sem("gates_ready")
        gate_biased = sem("gate_biased")
        gate_v = sem("gate_v")
        gate_a = sem("gate_a")
        cum_ready = sem("cum_ready")
        row_ready = sem("row_ready")
        ml_s_ready = sem("ml_s_ready")
        ml_free = sem("ml_free")
        max_ready = sem("max_ready")
        ml_w_ready = sem("ml_w_ready")
        ml_p_ready = sem("ml_p_ready")
        ml_t_ready = sem("ml_t_ready")
        ml_t_saved = sem("ml_t_saved")
        ml_h_ready = sem("ml_h_ready")
        ml_h_saved = sem("ml_h_saved")
        yb_ready = sem("yb_ready")
        yb_t_ready = sem("yb_t_ready")
        yb_hi = sem("yb_hi")
        yb_lo = sem("yb_lo")
        gn_in = sem("gn_in")
        na_s_ready = sem("na_s_ready")
        na_max = sem("na_max")
        na_exp = sem("na_exp")
        na_p = sem("na_p")
        na_t_ready = sem("na_t_ready")
        na_t_saved = sem("na_t_saved")
        na_o_ready = sem("na_o_ready")
        ya_hi = sem("ya_hi")
        ya_lo = sem("ya_lo")
        taps_in = sem("taps_in")
        z_hi = sem("z_hi")
        z_lo = sem("z_lo")
        out_done = sem("out_done")

        block = ctx.enter_context(nc.Block())

        def batch_bank(m):
            return psum[:, 4 + m % 2, :]

        def wait_batch_bank(e, m):
            if m >= 2:
                e.wait_ge(tp_lo, m - 1)

        @block.sync
        def _(sp):
            def fill_x(t, c):
                sp.dma_start(xs[:, t, c * 512:(c + 1) * 512],
                             x[0, t * P:(t + 1) * P, c * 512:(c + 1) * 512]).then_inc(x_in[2 * t + c], 16)

            fill_x(0, 0)
            fill_x(0, 1)

            def fill(g, slot):
                if not isinstance(g, int) or g >= RING:
                    sp.wait_ge(lo_made, g - RING + 1)
                sp.dma_start(raw[:, slot, :], weights[bass.ds(g * P, P), :]).then_inc(raw_in[slot], FILL)

            for g, i in FIRST_TILES:
                sp.dma_start(raw[:, g, tile_cols(i)], weights[g * P:(g + 1) * P, tile_cols(i)]).then_inc(
                    tile_in[g * TILES + i] if i < TILES - 1 else raw_in[g], FILL)
            fill_x(1, 0)
            fill_x(1, 1)
            fill(2, 2)
            fill(3, 3)
            with sp.Fori(1, GROUPS // RING) as it:
                for slot in range(RING):
                    fill(it * RING + slot, slot)
            for g in range(GROUPS // RING * RING, GROUPS):
                fill(g, g % RING)

            for t in range(NT):
                for c in range(2):
                    sp.wait_ge(x_ready, 4 * LAST + 2 * t + c + 1)
                    sp.dma_start(out[0, t * P:(t + 1) * P, c * 512:(c + 1) * 512],
                                 xs[:, t, c * 512:(c + 1) * 512]).then_inc(out_done, 16)
            sp.wait_ge(out_done, 16 * 4)

        @block.gpsimd
        def _(pool):
            nc.gpsimd.memset(minus_half[:, :], -0.5).then_inc(p_step, 1)
            pool.wait_ge(lo_made, 4)
            pool.dma_start(cst[:, P:], consts[:, P:]).then_inc(cst_in, 16)
            pool.dma_start(wg[:, :, :], gate_w).then_inc(wg_in, 16)
            pool.dma_start(gate_bias[:, :],
                           bass.AP(ab_gate_b.tensor, 0, [[1, N_GATES], [1, 1]])).then_inc(wg_in, 16)
            pool.dma_start(taps[:, :, :], conv_taps).then_inc(taps_in, 16)
            pool.wait_ge(p_step, 1)
            done = 0

            def rsqrt(n):
                nonlocal done
                done += 1
                pool.wait_ge(var_ready, done)
                nc.gpsimd.tensor_tensor(rstd[:, 0:n], var_eps[:, 0:n], minus_half[:, 0:n],
                                        ALU.pow).then_inc(rstd_ready, 1)

            for phase, (kind, _, _) in enumerate(PHASES):
                if phase:
                    pool.wait_ge(x_ready, 4 * phase)

                def norm_rows():
                    layer, i = divmod(phase, 3)
                    for j, v in enumerate((ln_g, ln_b)):
                        pool.dma_start(gb[:, j, :], v[layer, i, :].partition_broadcast(P)).then_inc(gb_in, 16)

                if kind != MIX:
                    norm_rows()
                else:
                    pool.wait_ge(acc_ready, 4 * phase)
                    for r2 in range(2):
                        for j in range(6):
                            first = (5 - r2 + j) * RPB_C + RPB_C // 2 - (GRID_W - 1)
                            pool.dma_start(rpb[64 * r2:64 * r2 + 64, :, j, :],
                                           bass.AP(na_rpb.tensor, first,
                                                   [[1, 64], [RPB_R * RPB_C, NA_H], [1, GRID_W]])
                                           ).then_inc(rpb_in, 16)
                    pool.dma_start(gn_gain[:, :], ml_gn_g[0].partition_broadcast(P)).then_inc(gn_in, 16)
                    pool.wait_ge(rpb_in, 16 * 12)
                    pool.wait_ge(cst_in, 16)
                    v = rpb[:, :, :, :].rearrange("p h j c -> p (h j) c")
                    nc.gpsimd.tensor_tensor(v, v, mask_na.unsqueeze(1).to_broadcast([P, NA_H * 6, GRID_W]),
                                            ALU.add).then_inc(rpb_made, 1)
                    pool.wait_ge(na_s_ready, NA_H)
                    norm_rows()
                    rsqrt(8)
                for t in range(NT):
                    rsqrt(1)

        @block.tensor
        def _(pe):
            mm = nc.tensor.matmul

            def split_mm(ps, s_hi, s_lo, m_hi, m_lo, first, last):
                mm(ps, s_hi, m_hi, start=first, stop=False)
                mm(ps, s_hi, m_lo, start=False, stop=False)
                return mm(ps, s_lo, m_hi, start=False, stop=last)

            def tile(slot, i):
                return w_hi[:, slot, i * 512:(i + 1) * 512], w_lo[:, slot, i * 512:(i + 1) * 512]

            def transposes(m, blocks):
                for i, b in enumerate(blocks):
                    last = nc.tensor.transpose(batch_bank(m)[:, i * P:(i + 1) * P], b, ident)
                last.then_inc(tp_ready, 1)

            def x_transposes(phase, t):
                for c in range(2):
                    m = x_batch(phase) + 2 * t + c
                    if phase == 0:
                        pe.wait_ge(x_in[m], 16)
                        pe.wait_ge(ident_in, 16)
                    else:
                        pe.wait_ge(x_ready, 4 * (phase - 1) + 2 * t + c + 1)
                    wait_batch_bank(pe, m)
                    transposes(m, [xs[:, t, (4 * c + k) * P:(4 * c + k + 1) * P] for k in range(4)])


            def natural_step(par, slots, g, after=None, new_x=None):
                for t in range(NT):
                    for c in range(2):
                        by_tile = new_x == 0 and t == 0
                        if t == 0 and not by_tile:
                            pe.wait_ge(lo_made, g + 1 + c)
                        if new_x is not None:
                            pe.wait_ge(tp_hi, x_batch(new_x) + 2 * t + c + 1)
                        tok = slice(t * P, (t + 1) * P)
                        ps = pair(par)[:, t, :]
                        for i in range(4):
                            hi, lo = tile(slots[c], i)
                            if by_tile:
                                if i < TILES - 1:
                                    pe.wait_ge(tile_lo, c * (TILES - 1) + i + 1)
                                else:
                                    pe.wait_ge(lo_made, c + 1)
                            mm(ps, xT_hi[:, 4 * c + i, tok], hi, start=(c, i) == (0, 0), stop=False)
                            mm(ps, xT_hi[:, 4 * c + i, tok], lo, start=False, stop=False)
                        if new_x is not None:
                            pe.wait_ge(tp_lo, x_batch(new_x) + 2 * t + c + 1)
                        for i in range(4):
                            hi, _ = tile(slots[c], i)
                            last = mm(ps, xT_lo[:, 4 * c + i, tok], hi, start=False, stop=(c, i) == (1, 3))
                        if (t, c) == (1, 0):
                            last.then_inc(group_used, 1)
                        if (t, c) == (0, 1):
                            last.then_inc(proj_ready, 1)
                        if after and (t, c) != (1, 1):
                            after(2 * t + c)
                return last

            def transposed_part(ps, slot, blk, ks):
                for k in ks:
                    hi, lo = tile(slot, k % 4)
                    mm(ps, hi[:, blk], xT_hi[:, k, :], start=k == 0, stop=False)
                    mm(ps, hi[:, blk], xT_lo[:, k, :], start=False, stop=False)
                    last = mm(ps, lo[:, blk], xT_hi[:, k, :], start=False, stop=k == KB - 1)
                return last

            def transposed_step(par, slots, g, after=None, new_x=None):
                pe.wait_ge(lo_made, g + 2)
                for b in range(4):
                    for c in range(2):
                        if new_x is not None and b == 0:
                            pe.wait_ge(tp_lo, x_batch(new_x) + 3 + c)
                        last = transposed_part(pair(par)[:, b // 2, (b % 2) * S:(b % 2 + 1) * S],
                                               slots[c], slice(b * P, (b + 1) * P),
                                               range(4 * c, 4 * c + 4))
                        if (b, c) == (3, 0):
                            last.then_inc(group_used, 1)
                    if b == 1:
                        last.then_inc(proj_ready, 1)
                    if after and b < 3:
                        after(b)
                return last

            def output(phase, hi, lo, wait_pair, wait_blocks, after=None):
                g0 = GROUP0[phase] + 2 * PHASES[phase][1]
                n_groups = PHASES[phase][2] // 2
                banks = [pair(acc_pair(phase)), psum[:, 6:8, :]]

                def block_mm(j, kk, t, c):
                    kb = 2 * j + kk
                    tok = slice(t * P, (t + 1) * P)
                    w1, w2 = tile((g0 + j) % RING, 2 * kk + c)
                    return split_mm(banks[t][:, c, :], hi(kb)[:, tok], lo(kb)[:, tok], w1, w2,
                                    kb == 0, kb == 2 * n_groups - 1)

                wait_pair()
                for j in range(n_groups - 2):
                    pe.wait_ge(lo_made, g0 + j + 1)
                    wait_blocks(j)
                    for kk in range(2):
                        for t in range(NT):
                            for c in range(2):
                                last = block_mm(j, kk, t, c)
                            if (kk, t) == (1, 1):
                                last.then_inc(group_used, 1)
                            if after:
                                after(j, 2 * kk + t)
                pe.wait_ge(lo_made, g0 + n_groups)
                for t in range(NT):
                    for c in range(2):
                        for j in range(n_groups - 2, n_groups):
                            if (t, c) == (0, 0):
                                wait_blocks(j)
                            for kk in range(2):
                                last = block_mm(j, kk, t, c)
                            if (t, c) == (1, 1) and j == n_groups - 2:
                                last.then_inc(group_used, 1)
                        last.then_inc(acc_ready, 1)

            def ffn(phase):
                g0, n0, m0 = GROUP0[phase], STEP0[phase], BATCH0[phase]
                h0 = sum(k == FFN for k, _, _ in PHASES[:phase]) * FSTEPS

                def hid_transposes(par, h_count, m_wait, bank):
                    pe.wait_ge(hid_ready, h_count)
                    pe.wait_ge(tp_lo, m_wait)
                    for i in range(4):
                        kk, t = divmod(i, 2)
                        last = nc.tensor.transpose(psum[:, 4 + bank, i * P:(i + 1) * P],
                                                   hid[:, par, t, kk * P:(kk + 1) * P], ident)
                    last.then_inc(tp_ready, 1)

                def step(s, off=0):
                    par = (n0 + off) % 2
                    g = s * 2 + (g0 + 2 * off)
                    slots = [(g0 + 2 * off) % RING, (g0 + 2 * off + 1) % RING]
                    first = isinstance(s, int) and s + off == 0
                    if not isinstance(s, int) or s + off >= 2:
                        pe.wait_ge(hid_ready, s + (h0 + off - 1))

                    def between():
                        lo0 = m0
                        hid_transposes((off + 1) % 2, s + (h0 + off), s + (lo0 + off - 2),
                                       (m0 + off - 1) % 2)

                    def after(q):
                        if q == 1:
                            x_transposes(phase, 1) if first else between()

                    natural_step(par, slots, g, after, phase if first else None).then_inc(proj_ready, 1)

                x_transposes(phase, 0)
                step(0, 0)
                step(0, 1)
                with pe.Fori(1, (FSTEPS - 1) // 2) as it:
                    for off in range(2):
                        step(it * 2, off)
                step(FSTEPS - 1, 0)
                lo0 = m0 + 1

                def last_transposes(j, q):
                    s = FSTEPS
                    if (j, q) == (0, 3):
                        hid_transposes((s + 1) % 2, h0 + s, lo0 + s - 3, (m0 + s - 1) % 2)

                output(phase, lambda kb: hT_hi[:, kb, :], lambda kb: hT_lo[:, kb, :],
                       lambda: pe.wait_ge(hid_ready, h0 + FSTEPS - 1), lambda j: pe.wait_ge(tp_lo, lo0 + j), last_transposes)

            def mix(phase):
                g0, n0, m0 = GROUP0[phase], STEP0[phase], BATCH0[phase]

                def step(i):
                    if i >= 2:
                        pe.wait_ge(proj_saved, i - 1)
                    slots = [(g0 + 2 * i) % RING, (g0 + 2 * i + 1) % RING]
                    f = transposed_step if MIX_COLS[i] in TRANSPOSED else natural_step
                    f((n0 + i) % 2, slots, g0 + 2 * i, lambda q: small_work(i, q),
                      None if i else phase).then_inc(proj_ready, 1)
                    small_work(i, 3)

                def gates():
                    pe.wait_ge(tp_lo, x_batch(phase) + 4)
                    pe.wait_ge(wg_split, 2)
                    for k in range(KB):
                        last = split_mm(psum[0:N_GATES, 4, 0:S], wg_hi[:, k, :], wg_lo[:, k, :],
                                        xT_hi[:, k, :], xT_lo[:, k, :], k == 0, k == KB - 1)
                    last.then_inc(gates_ready, 1)

                def gate_transposes():
                    pe.wait_ge(gate_biased, 1)
                    for t in range(NT):
                        last = nc.tensor.transpose(psum[:, 5, t * N_GATES:(t + 1) * N_GATES],
                                                   gates_T[:, t * P:(t + 1) * P],
                                                   ident[0:N_GATES, 0:N_GATES])
                    last.then_inc(gates_ready, 1)

                def cumulate():
                    pe.wait_ge(gate_v, 2)
                    pe.wait_ge(cst_in, 16)
                    cum = psum[:, 4, 0:16].rearrange("p (t d h) -> p t d h", t=2, d=2)
                    lf = small[:, 0, :].rearrange("p (t d h) -> p t d h", t=2, d=2)
                    mm(cum[:, 0, 0, :], tri_f, lf[:, 0, 0, :], start=True, stop=True)
                    mm(cum[:, 1, 0, :], ones, lf[:, 0, 0, :], start=True, stop=False)
                    mm(cum[:, 1, 0, :], tri_f, lf[:, 1, 0, :], start=False, stop=True)
                    mm(cum[:, 1, 1, :], tri_b, lf[:, 1, 1, :], start=True, stop=True)
                    mm(cum[:, 0, 1, :], ones, lf[:, 1, 1, :], start=True, stop=False)
                    mm(cum[:, 0, 1, :], tri_b, lf[:, 0, 1, :], start=False, stop=True).then_inc(cum_ready, 1)

                def rows_of(h):
                    r = small[:, 1, :].rearrange("p (t d h) -> p t d h", t=2, d=2)
                    pe.wait_ge(gate_v, 3)
                    if h:
                        pe.wait_ge(ml_free, h)
                    for d in range(2):
                        for t in range(NT):
                            c = (2 * d + t) * P
                            last = mm(psum[:, 7, c:c + P], r[:, t, d, h:h + 1].to_broadcast([P, P]), ident,
                                      start=True, stop=True)
                    last.then_inc(row_ready, 1)

                def qk(h):
                    pe.wait_ge(proj_saved, 5)
                    if h == 1:
                        pe.wait_ge(na_max, NA_H)
                    pe.wait_ge(ml_free, 4 if h < 2 else 4 + h - 1)
                    for t in range(NT):
                        last = mm(psum[:, ml_bank(h), t * S:(t + 1) * S], q_ml[:, h, t * P:(t + 1) * P],
                                  k_ml[:, h, :], start=True, stop=True)
                    last.then_inc(ml_s_ready, 1)

                def weights_T(h):
                    pe.wait_ge(ml_p_ready, h + 1)
                    if h == 0:
                        pe.wait_ge(na_t_saved, NA_H)
                    else:
                        pe.wait_ge(ml_t_saved, h)
                    for sh in range(2):
                        for t in range(NT):
                            last = nc.tensor.transpose(psum[:, 4, (2 * sh + t) * P:(2 * sh + t + 1) * P],
                                                       score[:, h, t * S + sh * P:t * S + (sh + 1) * P], ident)
                    last.then_inc(ml_t_ready, 1)

                def pv(h):
                    pe.wait_ge(ml_t_saved, h + 1)
                    pe.wait_ge(proj_saved, 6)
                    if h == 0:
                        pe.wait_ge(ya_lo, 4)
                        pe.wait_ge(ml_free, 8)
                    if h >= 2:
                        pe.wait_ge(ml_h_saved, h - 1)
                    for t in range(NT):
                        for sh in range(2):
                            last = mm(psum[:, 6 + h % 2, t * P:(t + 1) * P],
                                      p_ml[:, h % 2, sh, t * P:(t + 1) * P],
                                      v_ml[:, sh, h * ML_D:(h + 1) * ML_D], start=sh == 0, stop=sh == 1)
                    last.then_inc(ml_h_ready, 1)

                def output_T(i):
                    pe.wait_ge(yb_ready, i + 1)
                    if i == 0:
                        pe.wait_ge(ml_t_saved, ML_H)
                    for hh in range(2):
                        for t in range(NT):
                            last = nc.tensor.transpose(psum[:, 4 + i, (2 * hh + t) * P:(2 * hh + t + 1) * P],
                                                       h_ml[:, t, (2 * i + hh) * P:(2 * i + hh + 1) * P], ident)
                    last.then_inc(yb_t_ready, 1)

                def na_scores(h):
                    blk, po = h // 2, 64 * (h % 2)
                    if h == 0:
                        pe.wait_ge(proj_saved, 3)
                    else:
                        pe.wait_ge(na_max, h)
                    for t in range(NT):
                        last = mm(psum[:, 5, t * S:(t + 1) * S], q_na[po:po + 64, blk, t * P:(t + 1) * P],
                                  k_na[po:po + 64, blk, :], start=True, stop=True)
                    last.then_inc(na_s_ready, 1)

                def na_transposes(h):
                    pe.wait_ge(na_p, h + 1)
                    if h:
                        pe.wait_ge(na_t_saved, h)
                    for kh in range(2):
                        for t in range(NT):
                            last = nc.tensor.transpose(psum[:, 4, (2 * kh + t) * P:(2 * kh + t + 1) * P],
                                                       na_s[:, h % 2, t * S + kh * P:t * S + (kh + 1) * P], ident)
                    last.then_inc(na_t_ready, 1)

                def na_pv(h):
                    blk, po = h // 2, 64 * (h % 2)
                    pe.wait_ge(na_t_saved, h + 1)
                    if h % 2 == 0 and h:
                        pe.wait_ge(ya_lo, blk)
                    for kh in range(2):
                        last = mm(psum[po:po + 64, 6, 0:S], v_na[:, kh, h * NA_D:(h + 1) * NA_D],
                                  p_na[:, h % 2, kh, :], start=kh == 0, stop=kh == 1)
                    last.then_inc(na_o_ready, 1)

                def na_slot(k):
                    if 0 <= k - 2 < NA_H:
                        na_transposes(k - 2)
                    if k < NA_H:
                        na_scores(k)
                    if 0 <= k - 3 < NA_H:
                        na_pv(k - 3)

                def small_work(i, q):
                    at = 4 * i + q
                    if at == 1:
                        x_transposes(phase, 1)
                    if at == 3:
                        gates()
                    if at == 4:
                        gate_transposes()
                    if at == 6:
                        cumulate()
                    if at in ROW_QUARTERS:
                        rows_of(ROW_QUARTERS.index(at))
                    if 0 <= at - NA_QUARTER < NA_H + 3:
                        na_slot(at - NA_QUARTER)
                    if at in QK_QUARTERS:
                        qk(QK_QUARTERS.index(at))
                    if at == ML_QUARTER:
                        for h in range(ML_H):
                            weights_T(h)
                            if h:
                                pv(h - 1)
                        pv(ML_H - 1)

                x_transposes(phase, 0)
                for i in range(len(MIX_COLS)):
                    step(i)

                def wait_blocks(j):
                    if j == 0:
                        pe.wait_ge(ml_h_saved, ML_H)
                    if j == 2:
                        output_T(0)
                        output_T(1)
                    if j >= 2:
                        pe.wait_ge(yb_lo, j - 1)

                output(phase, lambda kb: (yaT_hi if kb < 4 else ybT_hi)[:, kb % 4, :],
                       lambda kb: (yaT_lo if kb < 4 else ybT_lo)[:, kb % 4, :],
                       lambda: pe.wait_ge(proj_saved, 7), wait_blocks)

            def conv(phase):
                g0, n0 = GROUP0[phase], STEP0[phase]
                x_transposes(phase, 0)
                x_transposes(phase, 1)
                for i in range(PHASES[phase][1]):
                    if i >= 2:
                        pe.wait_ge(conv_read, i - 1)
                    slots = [(g0 + 2 * i) % RING, (g0 + 2 * i + 1) % RING]
                    transposed_step((n0 + i) % 2, slots, g0 + 2 * i, None,
                                    None if i else phase).then_inc(proj_ready, 1)
                output(phase, lambda kb: zT_hi[:, kb, :], lambda kb: zT_lo[:, kb, :],
                       lambda: pe.wait_ge(conv_read, PHASES[phase][1] - 1),
                       lambda j: pe.wait_ge(z_lo, j // 2 + 1))

            for phase, (kind, _, _) in enumerate(PHASES):
                {FFN: ffn, MIX: mix, CONV: conv}[kind](phase)

        @block.scalar
        def _(act):
            copy = nc.scalar.copy
            act.dma_start(ident, consts[:, 0:P]).then_inc(ident_in, 16)

            counts = {"group": group_used, "proj": proj_ready, "acc": acc_ready}

            def split_hi(g, later=0):
                if g >= GROUPS:
                    return
                slot = g % RING
                act.wait_ge(raw_in[slot], later * FILL + (g // RING + 1) * FILL)
                if g >= RING:
                    which, value = USED[g - RING]
                    act.wait_ge(counts[which], later * {"group": 2, "proj": 4, "acc": 0}[which] + value)
                copy(w_hi[:, slot, :], raw[:, slot, :]).then_inc(hi_made, 1)

            def batch_hi(m, dst, view):
                act.wait_ge(tp_ready, m + 1)
                copy(dst, view(batch_bank(m))).then_inc(tp_hi, 1)

            def x_in_phase(phase):
                m = x_batch(phase)
                for t in range(NT):
                    for c in range(2):
                        batch_hi(m, xT_hi[:, 4 * c:4 * c + 4, t * P:(t + 1) * P],
                                 lambda b: b.rearrange("p (k n) -> p k n", k=4))
                        m += 1
                    if t == 0:
                        if phase == 0:
                            for g, i in FIRST_TILES:
                                act.wait_ge(tile_in[g * TILES + i] if i < TILES - 1 else raw_in[g], FILL)
                                copy(w_hi[:, g, tile_cols(i)], raw[:, g, tile_cols(i)]).then_inc(
                                    tile_hi if i < TILES - 1 else hi_made, 1)
                        else:
                            split_hi(GROUP0[phase] - 1 + LEAD)
                if phase == 0:
                    split_hi(2)
                nc.scalar.mul(ax[:, :, :], xs[:, :, :], ALPHA).then_inc(ax_ready, 1)

            def ffn(phase):
                g0, n0, m0 = GROUP0[phase], STEP0[phase], BATCH0[phase]
                h0 = sum(k == FFN for k, _, _ in PHASES[:phase]) * FSTEPS
                lo0 = m0

                def evacuate(s, off):
                    par = (n0 + off) % 2
                    act.wait_ge(proj_ready, s * 2 + (2 * (n0 + off) + 2))
                    act.wait_ge(tp_ready, s + (m0 + off - 1))
                    nc.scalar.activation(hid[:, off % 2, :, :], pair(par)[:, :, 0:256],
                                         ACT.Silu).then_inc(silu_ready, 1)

                def hid_hi(s, off):
                    act.wait_ge(tp_ready, s + (m0 + off + 1))
                    copy(hT_hi[:, bass.ds(s * 2 + 2 * off, 2), :],
                         psum[:, 4 + (m0 + off) % 2, :].rearrange("p (k n) -> p k n", k=2)
                         ).then_inc(tp_hi, 1)

                x_in_phase(phase)
                split_hi(g0 + LEAD)
                split_hi(g0 + 1 + LEAD)
                for off in (1, 2):
                    evacuate(0, off - 1)
                    split_hi(g0 + 2 * off + LEAD)
                    hid_hi(0, off - 1)
                    split_hi(g0 + 2 * off + 1 + LEAD)
                with act.Fori(1, (FSTEPS - 1) // 2) as it:
                    for off in (0, 1):
                        evacuate(it * 2, off)
                        g = g0 + 4 + 2 * (off + 1) + LEAD
                        split_hi(g, it - 1)
                        hid_hi(it * 2, off)
                        split_hi(g + 1, it - 1)
                g1 = g0 + 2 * FSTEPS
                evacuate(FSTEPS - 1, 0)
                split_hi(g1 + LEAD)
                hid_hi(FSTEPS - 1, 0)
                if phase == 0:
                    act.wait_ge(wg_in, 32)
                    copy(wg_hi[:, :, :], wg[:, :, :]).then_inc(wg_split, 1)
                for j in range(1, FKB // 2 - 1):
                    split_hi(g1 + j + LEAD)

            def mix(phase):
                g0, n0, m0 = GROUP0[phase], STEP0[phase], BATCH0[phase]
                dest = {"vb": v_ml[:, :, :], "ob": o_gate[:, :, :], "va": v_na[:, :, :], "qb": q_ml[:, :, :],
                        "kb": k_ml[:, :, :], "qa": q_na, "ka": k_na}

                def evacuate(i):
                    name = MIX_COLS[i]
                    act.wait_ge(proj_ready, 2 * (n0 + i) + 2)
                    src = pair((n0 + i) % 2)
                    dst = dest[name]
                    if name in TRANSPOSED:
                        src = src.rearrange("p b (c n) -> p (b c) n", c=2)
                    if name == "ob":
                        ins = nc.scalar.activation(dst, src, ACT.Sigmoid)
                    elif name == "qa":
                        ins = nc.scalar.mul(dst, src, float(NA_D) ** -0.5)
                    elif name == "kb":
                        ins = nc.scalar.mul(dst, src, float(ML_D) ** -0.5)
                    else:
                        ins = copy(dst, src)
                    ins.then_inc(proj_saved, 1)

                def ml_exp(h):
                    act.wait_ge(max_ready, 1)
                    for d in range(2):
                        for t in range(NT):
                            lo, hi = region(d, t)
                            k = (t * 2 + d) * ML_H + h
                            v = score[:, h, lo:hi]
                            last = nc.scalar.activation(v, v, ACT.Exp, bias=small[:, 6, k:k + 1])
                    last.then_inc(ml_w_ready, 1)

                def save_ml_T(h):
                    act.wait_ge(ml_t_ready, h + 1)
                    if h >= 2:
                        act.wait_ge(ml_h_ready, h - 1)
                    copy(p_ml[:, h % 2, :, :], psum[:, 4, :].rearrange("p (a n) -> p a n", a=2)
                         ).then_inc(ml_t_saved, 1)

                def save_h(h):
                    act.wait_ge(ml_h_ready, h + 1)
                    copy(h_ml[:, :, h * P:(h + 1) * P],
                         psum[:, 6 + h % 2, 0:S].rearrange("p (t n) -> p t n", t=2)
                         ).then_inc(ml_h_saved, 1)

                def yb_parts(i):
                    act.wait_ge(yb_t_ready, i + 1)
                    copy(ybT_hi[:, 2 * i:2 * i + 2, :], psum[:, 4 + i, :].rearrange("p (k n) -> p k n", k=2)
                         ).then_inc(yb_hi, 1)

                def na_exp_of(h):
                    act.wait_ge(na_max, h + 1)
                    for t in range(NT):
                        v = na_s[:, h % 2, t * S:(t + 1) * S]
                        c = 2 * h + t
                        last = nc.scalar.activation(v, v, ACT.Exp, bias=small[:, 10, c:c + 1],
                                                    accum_out=small[:, 11, c:c + 1])
                    last.then_inc(na_exp, 1)

                def save_na_T(h):
                    act.wait_ge(na_t_ready, h + 1)
                    if h >= 2:
                        act.wait_ge(na_o_ready, h - 1)
                    copy(p_na[:, h % 2, :, :], psum[:, 4, :].rearrange("p (a n) -> p a n", a=2)
                         ).then_inc(na_t_saved, 1)

                def out_hi(blk):
                    act.wait_ge(na_o_ready, 2 * blk + 2)
                    copy(yaT_hi[:, blk, :], psum[:, 6, 0:S]).then_inc(ya_hi, 1)

                def na_slot(k):
                    if 0 <= k - 2 < NA_H:
                        save_na_T(k - 2)
                    if k < NA_H:
                        na_exp_of(k)
                    if k >= 4 and k % 2 == 0:
                        out_hi((k - 4) // 2)

                x_in_phase(phase)
                split_hi(g0 + LEAD)
                split_hi(g0 + 1 + LEAD)
                for i in range(1, 7):
                    evacuate(i - 1)
                    for q in range(4):
                        if (i, q) == (1, 1):
                            act.wait_ge(gate_v, 1)
                            nc.scalar.activation(small[:, 3, :], small[:, 2, :], ACT.Exp).then_inc(gate_a, 1)
                            act.wait_ge(gate_a, 1)
                            nc.scalar.activation(small[:, 4, :], small[:, 3, :], ACT.Ln,
                                                 bias=1.0).then_inc(gate_a, 1)
                        if 0 <= 4 * i + q - NA_QUARTER < NA_H + 3:
                            na_slot(4 * i + q - NA_QUARTER)
                        if 4 * i + q in (16, 17, 20, 21):
                            ml_exp((16, 17, 20, 21).index(4 * i + q))
                        if 4 * i + q == 22:
                            act.wait_ge(gate_v, 4)
                            nc.scalar.activation(small[:, 8, :], small[:, 7, :], ACT.Exp,
                                                 scale=-1.0).then_inc(gate_a, 1)
                        for g in splits_after(i, q):
                            split_hi(g0 + g)
                evacuate(6)
                for h in range(ML_H):
                    save_ml_T(h)
                    if h:
                        save_h(h - 1)
                save_h(ML_H - 1)
                g1 = g0 + 14
                split_hi(g1 + LEAD)
                for i in range(2):
                    yb_parts(i)
                split_hi(g1 + 1 + LEAD)
                split_hi(g1 + 2 + LEAD)

            def conv(phase):
                g0, n0 = GROUP0[phase], STEP0[phase]
                x_in_phase(phase)
                n_steps = PHASES[phase][1]
                for i in range(n_steps + 1):
                    if i < n_steps:
                        split_hi(g0 + 2 * i + LEAD)
                        split_hi(g0 + 2 * i + 1 + LEAD)
                    if i in (3, 6):
                        j = i // 3 - 1
                        act.wait_ge(conv_read, i)
                        copy(zT_hi[:, 4 * j:4 * j + 4, :], zT[:, :, :]).then_inc(z_hi, 1)
                for j in range(KB // 2 - 1):
                    split_hi(g0 + 2 * n_steps + j + LEAD)

            for phase, (kind, _, _) in enumerate(PHASES):
                {FFN: ffn, MIX: mix, CONV: conv}[kind](phase)

        @block.vector
        def _(dve):
            vec = nc.vector
            steps = 0

            def wait_step_result():
                dve.wait_ge(v_step, steps)

            def counted(ins):
                nonlocal steps
                steps += 1
                ins.then_inc(v_step, 1)

            def split_lo(g, slot=None):
                if isinstance(g, int):
                    if g >= GROUPS:
                        return
                    slot = g % RING
                dve.wait_ge(hi_made, g + 1)
                vec.tensor_tensor(w_lo[:, slot, :], raw[:, slot, :], w_hi[:, slot, :].bitcast(F32),
                                  ALU.subtract).then_inc(lo_made, 1)

            def batch_lo(m, hi, dst, view):
                dve.wait_ge(tp_hi, m + 1)
                vec.tensor_tensor(dst, view(batch_bank(m)), hi.bitcast(F32), ALU.subtract).then_inc(tp_lo, 1)

            def x_lo(phase, t, c):
                a = (slice(None), slice(4 * c, 4 * c + 4), slice(t * P, (t + 1) * P))
                batch_lo(x_batch(phase) + 2 * t + c, xT_hi[a], xT_lo[a],
                         lambda b: b.rearrange("p (k n) -> p k n", k=4))

            rstds = 0

            def norm(phase, scale):
                banks = [pair(acc_pair(phase)), psum[:, 6:8, :]]
                dve.wait_ge(gb_in, 32 * (phase + 1))
                dve.wait_ge(ax_ready, phase + 1)

                def sums(t, c):
                    dve.wait_ge(acc_ready, 4 * phase + 2 * t + c + 1)
                    cs = slice(c * 512, (c + 1) * 512)
                    counted(vec.scalar_tensor_tensor(out=xs[:, t, cs], in0=banks[t][:, c, :], scalar=scale,
                                                     in1=ax[:, t, cs], op0=ALU.mult, op1=ALU.add))

                def half_moments(t, c):
                    wait_step_result()
                    counted(vec.bn_stats(stats[:, c, :], xs[:, t, c * 512:(c + 1) * 512]))

                def moments(t):
                    wait_step_result()
                    counted(vec.bn_aggr(mv[:, t, :], stats[:, :, :]))
                    wait_step_result()
                    vec.tensor_scalar(var_eps[:, 0:1], mv[:, t, 1:2], EPS, None, ALU.add).then_inc(var_ready, 1)

                def scaled(t):
                    nonlocal rstds
                    rstds += 1
                    for c in range(2):
                        cs = slice(c * 512, (c + 1) * 512)
                        counted(vec.scalar_tensor_tensor(out=xs[:, t, cs], in0=xs[:, t, cs],
                                                         scalar=mv[:, t, 0:1], in1=gb[:, 0, cs],
                                                         op0=ALU.subtract, op1=ALU.mult))
                    dve.wait_ge(rstd_ready, rstds)
                    for c in range(2):
                        cs = slice(c * 512, (c + 1) * 512)
                        dve.wait_ge(v_step, steps - 1 + c)
                        vec.scalar_tensor_tensor(out=xs[:, t, cs], in0=xs[:, t, cs], scalar=rstd[:, 0:1],
                                                 in1=gb[:, 1, cs], op0=ALU.mult,
                                                 op1=ALU.add).then_inc(x_ready, 1)

                for c in range(2):
                    sums(0, c)
                    half_moments(0, c)
                moments(0)
                scaled(0)
                for c in range(2):
                    sums(1, c)
                    if phase < LAST:
                        x_lo(phase + 1, 0, c)
                    half_moments(1, c)
                moments(1)
                scaled(1)
                if phase < LAST:
                    for c in range(2):
                        x_lo(phase + 1, 1, c)
                    split_lo(GROUP0[phase + 1] - 1 + LEAD)

            def ffn(phase):
                g0, n0, m0 = GROUP0[phase], STEP0[phase], BATCH0[phase]
                h0 = sum(k == FFN for k, _, _ in PHASES[:phase]) * FSTEPS
                lo0 = m0

                def hidden(s, off):
                    par = (n0 + off) % 2
                    dve.wait_ge(silu_ready, s + (h0 + off + 1))
                    vec.tensor_tensor(hid[:, off % 2, :, :], hid[:, off % 2, :, :], pair(par)[:, :, 256:512],
                                      ALU.mult).then_inc(hid_ready, 1)

                def hid_lo(s, off):
                    dve.wait_ge(tp_hi, s + (lo0 + off + 1))
                    dst = bass.ds(s * 2 + 2 * off, 2)
                    vec.tensor_tensor(hT_lo[:, dst, :],
                                      psum[:, 4 + (m0 + off) % 2, :].rearrange("p (k n) -> p k n", k=2),
                                      hT_hi[:, dst, :].bitcast(F32), ALU.subtract).then_inc(tp_lo, 1)

                split_lo(g0 + LEAD)
                split_lo(g0 + 1 + LEAD)
                for off in (1, 2):
                    hidden(0, off - 1)
                    split_lo(g0 + 2 * off + LEAD)
                    hid_lo(0, off - 1)
                    split_lo(g0 + 2 * off + 1 + LEAD)
                with dve.Fori(1, (FSTEPS - 1) // 2) as it:
                    for off in (0, 1):
                        hidden(it * 2, off)
                        g = g0 + 2 * (off + 1) + LEAD
                        split_lo(it * 4 + g, g % RING)
                        hid_lo(it * 2, off)
                        split_lo(it * 4 + (g + 1), (g + 1) % RING)
                g1 = g0 + 2 * FSTEPS
                hidden(FSTEPS - 1, 0)
                split_lo(g1 + LEAD)
                hid_lo(FSTEPS - 1, 0)
                if phase == 0:
                    dve.wait_ge(wg_split, 1)
                    vec.tensor_tensor(wg_lo[:, :, :], wg[:, :, :], wg_hi[:, :, :].bitcast(F32),
                                      ALU.subtract).then_inc(wg_split, 1)
                for j in range(1, FKB // 2 - 1):
                    split_lo(g1 + j + LEAD)
                norm(phase, 0.5)

            def mix(phase):
                nonlocal rstds
                dve.wait_ge(cst_in, 16)
                g0, n0, m0 = GROUP0[phase], STEP0[phase], BATCH0[phase]
                pre = small[:, 12:14, :]
                by = pre.rearrange("p t (d k h) -> p t d k h", d=2, k=2)
                flat = lambda row: small[:, row, :].rearrange("p (t d h) -> p t d h", t=2, d=2)

                def gate_rows():
                    dve.wait_ge(gates_ready, 2)
                    for t in range(NT):
                        counted(vec.tensor_copy(pre[:, t, :], psum[:, 5, t * N_GATES:(t + 1) * N_GATES]))
                    wait_step_result()
                    for t in range(NT):
                        f = by[:, t, :, 1, :]
                        last = vec.scalar_tensor_tensor(out=flat(2)[:, t], in0=f, scalar=-1.0, in1=f,
                                                        op0=ALU.mult, op1=ALU.min)
                    last.then_inc(gate_v, 1)

                def log_sigmoid():
                    dve.wait_ge(gate_a, 2)
                    for t in range(NT):
                        last = vec.scalar_tensor_tensor(out=flat(0)[:, t], in0=by[:, t, :, 1, :], scalar=0.0,
                                                        in1=flat(4)[:, t], op0=ALU.min, op1=ALU.subtract)
                    last.then_inc(gate_v, 1)

                def relative():
                    dve.wait_ge(cum_ready, 1)
                    counted(vec.tensor_copy(small[:, 5, :], psum[:, 4, 0:16]))
                    wait_step_result()
                    for t in range(NT):
                        last = vec.tensor_tensor(flat(1)[:, t], by[:, t, :, 0, :], flat(5)[:, t], ALU.subtract)
                    last.then_inc(gate_v, 1)

                def maxima(h):
                    dve.wait_ge(row_ready, h + 1)
                    for d in range(2):
                        for t in range(NT):
                            lo, hi = allowed(d, t)
                            r_lo, r_hi = region(d, t)
                            k = (t * 2 + d) * ML_H + h
                            mask = (mask_f if d == 0 else mask_b)
                            m_lo = mask_start(d, t)
                            last = vec.tensor_tensor_reduce(
                                score[:, h, r_lo:r_hi], psum[:, 7, d * S + lo:d * S + hi],
                                mask[:, m_lo:m_lo + hi - lo], 1.0, 0.0, ALU.add, ALU.max,
                                small[:, 14, k:k + 1])
                    last.then_inc(ml_free, 1)

                def stabilise():
                    dve.wait_ge(ml_free, 4)
                    vec.tensor_tensor(small[:, 7, :], small[:, 5, :], small[:, 14, :], ALU.add).then_inc(gate_v, 1)
                    vec.tensor_scalar(small[:, 6, :], small[:, 14, :], -1.0, None, ALU.mult).then_inc(max_ready, 1)

                def weigh(h):
                    dve.wait_ge(ml_s_ready, h + 1)
                    dve.wait_ge(ml_w_ready, h + 1)
                    for d in range(2):
                        for t in range(NT):
                            lo, hi = allowed(d, t)
                            r_lo, r_hi = region(d, t)
                            k = (t * 2 + d) * ML_H + h
                            v = score[:, h, r_lo:r_hi]
                            last = vec.tensor_tensor_reduce(
                                v, v, psum[:, ml_bank(h), t * S + lo:t * S + hi], 1.0, 0.0,
                                ALU.mult, ALU.add, small[:, 15, k:k + 1])
                    last.then_inc(ml_free, 1)

                def denominators():
                    dve.wait_ge(ml_free, 8)
                    counted(vec.scalar_tensor_tensor(out=small[:, 3, :], in0=small[:, 15, :], scalar=-1.0,
                                                     in1=small[:, 15, :], op0=ALU.mult, op1=ALU.max))
                    dve.wait_ge(gate_a, 3)
                    wait_step_result()
                    counted(vec.tensor_tensor(small[:, 4, :], small[:, 3, :], small[:, 8, :], ALU.max))
                    wait_step_result()
                    counted(vec.reciprocal(small[:, 9, :], small[:, 4, :]))
                    wait_step_result()

                def combine(h):
                    for t in range(NT):
                        full, part = 1 - t, t
                        kf = (t * 2 + full) * ML_H + h
                        kp = (t * 2 + part) * ML_H + h
                        whole = score[:, h, t * S:(t + 1) * S]
                        own = score[:, h, t * S + t * P:t * S + (t + 1) * P]
                        counted(vec.tensor_scalar(whole, whole, small[:, 9, kf:kf + 1], None, ALU.mult))
                        wait_step_result()
                        last = vec.scalar_tensor_tensor(
                            out=own, in0=score[:, h, 2 * S + t * P:2 * S + (t + 1) * P],
                            scalar=small[:, 9, kp:kp + 1], in1=own, op0=ALU.mult, op1=ALU.add)
                    last.then_inc(ml_p_ready, 1)

                def rpb_keys(h, j):
                    v = rpb[:, h, j:j + ROWS, :]
                    (pitch, n), (row, _), (one, _) = v.ap
                    return bass.AP(v.tensor, v.offset + GRID_W - 1, [[pitch, n], [row, ROWS], [-one, GRID_W]])

                def na_maxima(h):
                    if h == 0:
                        dve.wait_ge(rpb_made, 1)
                    dve.wait_ge(na_s_ready, h + 1)
                    if h >= 2:
                        dve.wait_ge(na_t_ready, h - 1)
                    for t in range(NT):
                        j = 2 - 2 * t
                        c = 2 * h + t
                        counted(vec.tensor_tensor_reduce(
                            na_s[:, h % 2, t * S:(t + 1) * S].rearrange("p (j c) -> p j c", j=ROWS),
                            psum[:, 5, t * S:(t + 1) * S].rearrange("p (j c) -> p j c", j=ROWS),
                            rpb_keys(h, j), 1.0, -3e38, ALU.add, ALU.max, small[:, 12, c:c + 1]))
                    wait_step_result()
                    vec.tensor_scalar(small[:, 10, 2 * h:2 * h + 2], small[:, 12, 2 * h:2 * h + 2], -1.0, None,
                                      ALU.mult).then_inc(na_max, 1)

                def na_norm(h):
                    dve.wait_ge(na_exp, h + 1)
                    counted(vec.reciprocal(small[:, 13, 2 * h:2 * h + 2], small[:, 11, 2 * h:2 * h + 2]))
                    wait_step_result()
                    for t in range(NT):
                        v = na_s[:, h % 2, t * S:(t + 1) * S]
                        c = 2 * h + t
                        last = vec.tensor_scalar(v, v, small[:, 13, c:c + 1], None, ALU.mult)
                    last.then_inc(na_p, 1)

                def out_lo(blk):
                    dve.wait_ge(ya_hi, blk + 1)
                    vec.tensor_tensor(yaT_lo[:, blk, :], psum[:, 6, 0:S],
                                      yaT_hi[:, blk, :].bitcast(F32), ALU.subtract).then_inc(ya_lo, 1)

                def na_slot(k):
                    if k < NA_H:
                        na_maxima(k)
                    if k >= 4 and k % 2 == 0:
                        out_lo((k - 4) // 2)
                    if 0 <= k - 1 < NA_H:
                        na_norm(k - 1)

                split_lo(g0 + LEAD)
                split_lo(g0 + 1 + LEAD)
                dve.wait_ge(gates_ready, 1)
                vec.tensor_scalar(gates_T[:, :], psum[0:N_GATES, 4, 0:S], gate_bias[:, 0:1], None,
                                  ALU.add).then_inc(gate_biased, 1)
                for i in range(1, 7):
                    for q in range(4):
                        at = 4 * i + q
                        if at == 4:
                            gate_rows()
                        if at == 5:
                            log_sigmoid()
                        if at == 6:
                            relative()
                        if at in ROW_QUARTERS:
                            maxima(ROW_QUARTERS.index(at))
                        if at == ROW_QUARTERS[-1]:
                            stabilise()
                        if 0 <= at - NA_QUARTER < NA_H + 3:
                            na_slot(at - NA_QUARTER)
                        if at in QK_QUARTERS:
                            weigh(QK_QUARTERS.index(at))
                        if at == QK_QUARTERS[-1]:
                            denominators()
                            combine(0)
                            combine(1)
                        for g in splits_after(i, q):
                            split_lo(g0 + g)
                combine(2)
                combine(3)

                st = norm_stats[:, :, 0:6]
                agg = norm_stats[:, :, 6:8]
                dve.wait_ge(gn_in, 16)
                dve.wait_ge(proj_saved, 7)
                for t in range(NT):
                    counted(vec.tensor_tensor(o_gate[:, t, :], o_gate[:, t, :], gn_gain[:, :], ALU.mult))
                for h in range(ML_H):
                    dve.wait_ge(ml_h_saved, h + 1)
                    for t in range(NT):
                        counted(vec.bn_stats(st[:, t * 4 + h, :], h_ml[:, t, h * P:(h + 1) * P]))
                wait_step_result()
                for i in range(8):
                    counted(vec.bn_aggr(agg[:, i, :], st[:, i, :]))
                wait_step_result()
                vec.tensor_scalar(var_eps[:, 0:8], agg[:, :, 1], EPS, None, ALU.add).then_inc(var_ready, 1)
                rstds += 1
                split_lo(g0 + 14 + LEAD)
                dve.wait_ge(rstd_ready, rstds)
                for i in range(2):
                    for h in (2 * i, 2 * i + 1):
                        for t in range(NT):
                            k = t * 4 + h
                            v = h_ml[:, t, h * P:(h + 1) * P]
                            counted(vec.tensor_scalar(v, v, agg[:, k, 0:1], rstd[:, k:k + 1],
                                                      ALU.subtract, ALU.mult))
                    wait_step_result()
                    cs = slice(2 * i * P, (2 * i + 2) * P)
                    vec.tensor_tensor(h_ml[:, :, cs], h_ml[:, :, cs], o_gate[:, :, cs],
                                      ALU.mult).then_inc(yb_ready, 1)
                for i in range(2):
                    dve.wait_ge(yb_hi, i + 1)
                    vec.tensor_tensor(ybT_lo[:, 2 * i:2 * i + 2, :],
                                      psum[:, 4 + i, :].rearrange("p (k n) -> p k n", k=2),
                                      ybT_hi[:, 2 * i:2 * i + 2, :].bitcast(F32), ALU.subtract).then_inc(yb_lo, 1)
                split_lo(g0 + 15 + LEAD)
                split_lo(g0 + 16 + LEAD)
                norm(phase, 1.0)

            def conv(phase):
                g0, n0 = GROUP0[phase], STEP0[phase]
                counted(vec.memset(uT[:, :, 0:1], 0.0))
                counted(vec.memset(uT[:, :, S + 1:S + 2], 0.0))
                split_lo(g0 + LEAD)
                split_lo(g0 + 1 + LEAD)
                dve.wait_ge(taps_in, 16)
                n_steps = PHASES[phase][1]
                for i in range(n_steps):
                    part, j = CONV_STEPS[i]
                    src = pair((n0 + i) % 2).rearrange("p b (c n) -> p (b c) n", c=2)
                    dve.wait_ge(proj_ready, 2 * (n0 + i) + 2)
                    if part == 1:
                        vec.tensor_copy(cgT[:, :, :], src).then_inc(conv_read, 1)
                    if part == 2:
                        dve.wait_ge(conv_read, i)
                        vec.tensor_tensor(uT[:, :, 1:S + 1], src, cgT[:, :, :], ALU.mult).then_inc(conv_read, 1)
                        dve.wait_ge(conv_read, i + 1)
                        wait_step_result()
                        for tap in (1, 0, 2):
                            for b in range(4):
                                w = taps[:, 4 * j + b, :]
                                u = uT[:, b, tap:tap + S]
                                if tap == 1:
                                    counted(vec.tensor_scalar(yT[:, b, :], u, w[:, 1:2], w[:, 3:4],
                                                              ALU.mult, ALU.add))
                                else:
                                    dve.wait_ge(v_step, steps - 3)
                                    counted(vec.scalar_tensor_tensor(out=yT[:, b, :], in0=u,
                                                                     scalar=w[:, tap:tap + 1], in1=yT[:, b, :],
                                                                     op0=ALU.mult, op1=ALU.add))
                    if part == 0:
                        wait_step_result()
                        if j == 1:
                            dve.wait_ge(z_hi, 1)
                        vec.tensor_tensor(zT[:, :, :], src, yT[:, :, :], ALU.mult).then_inc(conv_read, 1)
                    if i + 1 < n_steps:
                        split_lo(g0 + 2 * (i + 1) + LEAD)
                        split_lo(g0 + 2 * (i + 1) + 1 + LEAD)
                    if part == 0:
                        dve.wait_ge(z_hi, j + 1)
                        vec.tensor_tensor(zT_lo[:, 4 * j:4 * j + 4, :], zT[:, :, :],
                                          zT_hi[:, 4 * j:4 * j + 4, :].bitcast(F32),
                                          ALU.subtract).then_inc(z_lo, 1)
                for j in range(KB // 2 - 1):
                    split_lo(g0 + 2 * n_steps + j + LEAD)
                norm(phase, 1.0)

            x_lo(0, 0, 0)
            x_lo(0, 0, 1)
            for g, i in FIRST_TILES:
                if i < TILES - 1:
                    dve.wait_ge(tile_hi, g * (TILES - 1) + i + 1)
                else:
                    dve.wait_ge(hi_made, g + 1)
                vec.tensor_tensor(w_lo[:, g, tile_cols(i)], raw[:, g, tile_cols(i)],
                                  w_hi[:, g, tile_cols(i)].bitcast(F32),
                                  ALU.subtract).then_inc(tile_lo if i < TILES - 1 else lo_made, 1)
            x_lo(0, 1, 0)
            x_lo(0, 1, 1)
            split_lo(2)
            for phase, (kind, _, _) in enumerate(PHASES):
                {FFN: ffn, MIX: mix, CONV: conv}[kind](phase)


_INS = ["x", "ln_g", "ln_b", "ab_gate_b", "na_rpb", "ml_gn_g"]


def weight_groups(ffn_w_in, ffn_w_out, ab_w_in, ab_w_out, sc_w_in, sc_w_out):
    groups = np.empty((GROUPS, P, TILES * 512), np.float32)
    at = 0

    def put(a):
        nonlocal at
        n = a.shape[0]
        groups[at:at + n].reshape(a.shape)[...] = a
        at += n

    def columns(w, c0):
        put(w[:, c0:c0 + 512].reshape(2, 4, P, 512).transpose(0, 2, 1, 3))

    def rows(w):
        put(w.reshape(-1, 2, P, D).transpose(0, 2, 1, 3))

    for phase, (kind, _, _) in enumerate(PHASES):
        layer, i = divmod(phase, 3)
        if kind == FFN:
            w = ffn_w_in[layer, i // 2].reshape(2, 4, P, 2, FSTEPS, 256).transpose(4, 0, 2, 1, 3, 5)
            for step in w:
                put(step)
            rows(ffn_w_out[layer, i // 2])
        elif kind == MIX:
            for name in MIX_COLS:
                columns(ab_w_in[0], 512 * MIX_AT[name])
            rows(ab_w_out[0])
        else:
            for part, half in CONV_STEPS:
                columns(sc_w_in[0], part * D + half * 512)
            rows(sc_w_out[0])
    return groups.reshape(GROUPS * P, TILES * 512)


def kernel(**inputs):
    import concourse.bacc as bacc
    from concourse.bass_utils import run_bass_kernel_spmd

    nc = bacc.Bacc("TRN2", target_bir_lowering=False, num_devices=1)
    given = {n: np.asarray(a) for n, a in inputs.items()}
    laid_out = {n: given[n] for n in _INS}
    laid_out["na_rpb"] = given["na_rpb"][..., ::-1]
    laid_out["weights"] = weight_groups(*[given[n] for n in (
        "ffn_w_in", "ffn_w_out", "ab_w_in", "ab_w_out", "sc_w_in", "sc_w_out")])
    laid_out["gate_w"] = given["ab_w_in"][0, :, 7 * 512:].reshape(KB, P, N_GATES).transpose(1, 0, 2)
    laid_out["conv_taps"] = np.concatenate([given["sc_conv_w"][0], given["sc_conv_b"]]).reshape(
        4, KB, P).transpose(2, 1, 0)
    laid_out["consts"] = constants()
    arrays, args = {}, []
    for name, a in laid_out.items():
        a = np.ascontiguousarray(a)
        arrays[f"in_{name}"] = a
        args.append(nc.dram_tensor(f"in_{name}", a.shape, mybir.dt.from_np(a.dtype), kind="ExternalInput").ap())
    args.append(nc.dram_tensor("out_0", (1, S, D), F32, kind="ExternalOutput").ap())
    build(nc, *args)
    r = run_bass_kernel_spmd(nc, [arrays], core_ids=[0])
    return r.results[0]["out_0"]
```

```python
from contextlib import ExitStack

import numpy as np

import concourse.bass as bass
from concourse import mybir

ALU = mybir.AluOpType
ACT = mybir.ActivationFunctionType
F32 = mybir.dt.float32
F32R = mybir.dt.float32r

P = 128
D = 1024
S = 256
NT = S // P
KB = D // P
FF = 2816
FKB = FF // P
UNITS = FKB - 2
NA_H, NA_D = 8, 64
ML_H, ML_D = 4, 128
GRID_W, WIN_W = 64, 16
ROWS = S // GRID_W
RPB_R, RPB_C = 15, 31
N_GATES = 4 * ML_H
ALPHA = 4.0 ** 0.25
EPS = 1e-5
NEG = -1e30

RING = 4
TILES = 4
LEAD = 3
FILL = 16

FFN, MIX, CONV = "ffn", "mix", "conv"
MIX_COLS = ["va", "qa", "ka", "qb", "kb", "vb", "ob"]
MIX_AT = {n: i for i, n in enumerate(["qa", "ka", "va", "qb", "kb", "vb", "ob"])}
TRANSPOSED = ("qb", "kb", "qa", "ka")
_FFN = (FFN, 1 + UNITS, 2 + UNITS, FKB)
_MIX = (MIX, len(MIX_COLS), 2 * len(MIX_COLS), KB)
_CONV = (CONV, 3 * D // 512, 2 * (3 * D // 512), KB)
PHASES = [_FFN, _MIX, _FFN, _FFN, _CONV, _FFN]
CONV_STEPS = [(1, 0), (2, 0), (0, 0), (1, 1), (2, 1), (0, 1)]

USED = []
GROUP0, STEP0, BATCH0 = [], [], []
_g = _n = 0
_m = 4
for _kind, _steps, _groups, _kb in PHASES:
    GROUP0.append(_g)
    STEP0.append(_n)
    BATCH0.append(_m)
    _g += _groups + _kb // 2
    _n += _steps
    for _i in range(_steps):
        if _kind != FFN or _i == 0:
            USED.append(("group", sum(u[0] == "group" for u in USED) + 1))
        USED.append(("proj", 2 * (STEP0[-1] + _i) + 2))
    for _i in range(_kb // 2 - 1):
        USED.append(("group", sum(u[0] == "group" for u in USED) + 1))
    USED.append(("acc", 4 * len(GROUP0)))
    _m += (_kind == FFN) + 4
GROUPS = _g
LAST = len(PHASES) - 1
FIRST_TILES = [(g, i) for g in range(2) for i in range(TILES)]


def tile_cols(i):
    return slice(i * 512, (i + 1) * 512)


def x_batch(phase):
    return BATCH0[phase] - 4


def acc_pair(phase):
    return (STEP0[phase] + PHASES[phase][1]) % 2


ROW_QUARTERS = [7, 8, 9, 11]
NA_QUARTER = 12
QK_QUARTER = 20
ML_QUARTER = 24


def score_bank(h):
    return 7 if h % 2 else 5


def splits_after(i, q):
    groups = []
    if q == 0 and MIX_COLS[i - 1] in TRANSPOSED:
        groups.append(2 * (i - 1) + 1 + LEAD)
    if q == 0:
        groups.append(2 * i + LEAD)
    if q == 2 and MIX_COLS[i] not in TRANSPOSED:
        groups.append(2 * i + 1 + LEAD)
    return groups


def constants():
    s = np.arange(P)[:, None]
    t = np.arange(P)[None, :]
    cols = [np.eye(P), s <= t, s >= t, np.ones((P, P)),
            np.zeros((P, P)), np.where(t <= s, 0, NEG),
            np.where(t >= s, 0, NEG), np.zeros((P, P))]
    c = np.arange(P)[:, None] % GRID_W
    kc = np.arange(GRID_W)[None, :]
    start = np.clip(c - WIN_W // 2, 0, GRID_W - WIN_W)
    cols.append(np.where((kc >= start) & (kc < start + WIN_W), 0, NEG)[:, ::-1])
    return np.concatenate([np.asarray(a, np.float32) for a in cols], axis=1)


def region(d, t):
    return (t * S, (t + 1) * S) if t != d else (2 * S + t * P, 2 * S + (t + 1) * P)


def allowed(d, t):
    return (0, S) if t != d else (t * P, (t + 1) * P)


def mask_start(d, t):
    return P if (d, t) == (0, 0) else 0


CONST_W = 8 * P + GRID_W


def build(nc, x, ln_g, ln_b, ab_gate_b, na_rpb, ml_gn_g, weights, gate_w, conv_taps, consts, out):
    ctx = ExitStack()
    with ctx:
        def sem(name):
            return ctx.enter_context(nc.semaphore(name))

        def sb(name, shape, dt=F32):
            return ctx.enter_context(nc.sbuf_tensor(name, shape, dt))

        raw = sb("raw", [P, RING, TILES * 512])
        w_hi = sb("w_hi", [P, RING, TILES * 512], F32R)
        w_lo = sb("w_lo", [P, RING, TILES * 512], F32R)
        xs = sb("xs", [P, NT, D])
        ax = sb("ax", [P, NT, D])
        xT = sb("xT", [P, KB, NT, 2, P], F32R)
        xT_hi = xT[:, :, :, 0, :]
        xT_lo = xT[:, :, :, 1, :]
        gb = sb("gb", [P, 2, D])
        cst = sb("cst", [P, CONST_W])
        wg = sb("wg", [P, KB, N_GATES])
        wg_hi = sb("wg_hi", [P, KB, N_GATES], F32R)
        wg_lo = sb("wg_lo", [P, KB, N_GATES], F32R)
        gate_bias = sb("gate_bias", [N_GATES, 1])
        stats = sb("stats", [P, 2, 6])
        mv = sb("mv", [P, NT, 2])
        var_eps = sb("var_eps", [P, 8])
        rstd = sb("rstd", [P, 8])
        minus_half = sb("minus_half", [P, 8])
        small = sb("small", [P, 16, 16])
        ident = cst[:, 0:P]
        tri_f = cst[:, P:2 * P]
        tri_b = cst[:, 2 * P:3 * P]
        ones = cst[:, 3 * P:4 * P]
        mask_f = cst[:, 4 * P:6 * P]
        mask_b = cst[:, 6 * P:8 * P]
        mask_na = cst[:, 8 * P:8 * P + GRID_W]

        ARENA = 65792
        arena_at = -(-nc.sbuf_base // 32) * 32
        sb("arena", [P, ARENA // 4])
        at = {}

        def place(phase, name, shape, dt=F32):
            size = int(np.prod(shape[1:])) * 4
            offset = at.get(phase, 0)
            at[phase] = offset + size
            assert at[phase] <= ARENA, (phase, name, at[phase])
            return nc.alloc_sbuf_tensor_at(name, shape, dt, offset=arena_at + offset)

        hT_hi = place(FFN, "hT_hi", [P, FKB, S], F32R)
        hT_lo = place(FFN, "hT_lo", [P, FKB, S], F32R)
        hid = place(FFN, "hid", [P, NT, 256])
        unit_h = place(FFN, "unit_h", [P, 2, S])
        unit_u = place(FFN, "unit_u", [P, S])

        score = place(MIX, "score", [P, ML_H, 3 * S])
        yaT_hi = place(MIX, "yaT_hi", [P, 4, S], F32R)
        yaT_lo = place(MIX, "yaT_lo", [P, 4, S], F32R)
        q_ml = place(MIX, "q_ml", [P, 4, S])
        k_ml = place(MIX, "k_ml", [P, 4, S])
        ybT_hi = nc.alloc_sbuf_tensor_at("ybT_hi", [P, 4, S], F32R, offset=arena_at + at[MIX] - 8192)
        ybT_lo = nc.alloc_sbuf_tensor_at("ybT_lo", [P, 4, S], F32R, offset=arena_at + at[MIX] - 4096)
        q_na, k_na = (gb[:, j, :].rearrange("p (b n) -> p b n", b=4) for j in range(2))
        v_ml = place(MIX, "v_ml", [P, NT, 512])
        o_gate = place(MIX, "o_gate", [P, NT, 512])
        v_na = place(MIX, "v_na", [P, NT, 512])
        p_na = place(MIX, "p_na", [P, 2, NT, S])
        p_ml = place(MIX, "p_ml", [P, 2, NT, S])
        gates_T = nc.alloc_sbuf_tensor_at("gates_T", [N_GATES, S], F32,
                                          offset=arena_at + at[MIX] - 4096)
        rpb = place(MIX, "rpb", [P, NA_H, 6, GRID_W])
        gn_gain = place(MIX, "gn_gain", [P, 512])
        norm_stats = place(MIX, "norm_stats", [P, 8, 8])
        h_ml = xs[:, :, 0:512]
        na_third = place(MIX, "na_third", [P, 512])
        na_s = [xs[:, 0, 512:1024], xs[:, 1, 512:1024], na_third[:, :]]

        cgT = place(CONV, "cgT", [P, 4, S])
        cg_nat = place(CONV, "cg_nat", [P, NT, 512])
        uT = place(CONV, "uT", [P, 4, S + 2])
        yT = place(CONV, "yT", [P, 4, S])
        zT = place(CONV, "zT", [P, 4, S])
        zT_hi = place(CONV, "zT_hi", [P, KB, S], F32R)
        zT_lo = place(CONV, "zT_lo", [P, KB, S], F32R)
        taps = sb("taps", [P, KB, 4])

        psum = ctx.enter_context(nc.psum_tensor("psum", [P, 8, 512], F32))

        def pair(p):
            return psum[:, 2 * p:2 * p + 2, :]

        raw_in = [sem(f"raw_in{i}") for i in range(RING)]
        hi_made = sem("hi_made")
        lo_made = sem("lo_made")
        group_used = sem("group_used")
        proj_ready = sem("proj_ready")
        proj_saved = sem("proj_saved")
        conv_read = sem("conv_read")
        silu_ready = sem("silu_ready")
        hid_ready = sem("hid_ready")
        apart_saved = sem("apart_saved")
        gate_sum = sem("gate_sum")
        gate_silu = sem("gate_silu")
        up_sum = sem("up_sum")
        unit_ready = sem("unit_ready")
        unit_hi = sem("unit_hi")
        unit_lo = sem("unit_lo")
        tp_ready = sem("tp_ready")
        tp_hi = sem("tp_hi")
        tp_lo = sem("tp_lo")
        acc_ready = sem("acc_ready")
        x_ready = sem("x_ready")
        ax_ready = sem("ax_ready")
        var_ready = sem("var_ready")
        rstd_ready = sem("rstd_ready")
        v_step = sem("v_step")
        p_step = sem("p_step")
        x_in = [sem(f"x_in{i}") for i in range(2 * NT)]
        tile_in = [sem(f"tile_in{i}") for i in range(2 * TILES - 1)]
        tile_hi = sem("tile_hi")
        tile_lo = sem("tile_lo")
        ident_in = sem("ident_in")
        cst_in = sem("cst_in")
        gb_in = sem("gb_in")
        wg_in = sem("wg_in")
        wg_split = sem("wg_split")
        rpb_in = sem("rpb_in")
        rpb_made = sem("rpb_made")
        gates_ready = sem("gates_ready")
        gate_biased = sem("gate_biased")
        gate_v = sem("gate_v")
        gate_a = sem("gate_a")
        cum_ready = sem("cum_ready")
        row_ready = sem("row_ready")
        ml_s_ready = sem("ml_s_ready")
        ml_free = sem("ml_free")
        max_ready = sem("max_ready")
        ml_w_ready = sem("ml_w_ready")
        ml_p_ready = sem("ml_p_ready")
        ml_t_ready = sem("ml_t_ready")
        ml_t_saved = sem("ml_t_saved")
        ml_h_ready = sem("ml_h_ready")
        ml_h_saved = sem("ml_h_saved")
        yb_ready = sem("yb_ready")
        yb_t_ready = sem("yb_t_ready")
        yb_hi = sem("yb_hi")
        yb_lo = sem("yb_lo")
        gn_in = sem("gn_in")
        na_s_ready = sem("na_s_ready")
        na_max = sem("na_max")
        na_exp = sem("na_exp")
        na_p = sem("na_p")
        na_t_ready = sem("na_t_ready")
        na_t_saved = sem("na_t_saved")
        na_o_ready = sem("na_o_ready")
        ya_hi = sem("ya_hi")
        ya_lo = sem("ya_lo")
        taps_in = sem("taps_in")
        cg_t_ready = sem("cg_t_ready")
        cg_saved = sem("cg_saved")
        z_hi = sem("z_hi")
        z_lo = sem("z_lo")
        out_done = sem("out_done")

        block = ctx.enter_context(nc.Block())

        def batch_bank(m):
            return psum[:, 4 + m % 2, :]

        def wait_batch_bank(e, m):
            if m >= 2:
                e.wait_ge(tp_lo, m - 1)

        @block.sync
        def _(sp):
            def fill_x(t, c):
                sp.dma_start(xs[:, t, c * 512:(c + 1) * 512],
                             x[0, t * P:(t + 1) * P, c * 512:(c + 1) * 512]).then_inc(x_in[2 * t + c], 16)

            def fill(g, slot):
                if not isinstance(g, int) or g >= RING:
                    sp.wait_ge(lo_made, g - RING + 1)
                sp.dma_start(raw[:, slot, :], weights[bass.ds(g * P, P), :]).then_inc(raw_in[slot], FILL)

            fill_x(0, 0)
            for g, i in FIRST_TILES:
                if (g, i) == (0, 1):
                    fill_x(0, 1)
                sp.dma_start(raw[:, g, tile_cols(i)], weights[g * P:(g + 1) * P, tile_cols(i)]).then_inc(
                    tile_in[g * TILES + i] if i < TILES - 1 else raw_in[g], FILL)
            fill_x(1, 0)
            fill_x(1, 1)
            fill(2, 2)
            fill(3, 3)
            with sp.Fori(1, GROUPS // RING) as it:
                for slot in range(RING):
                    fill(it * RING + slot, slot)
            for g in range(GROUPS // RING * RING, GROUPS):
                fill(g, g % RING)

            for t in range(NT):
                for c in range(2):
                    sp.wait_ge(x_ready, 4 * LAST + 2 * t + c + 1)
                    sp.dma_start(out[0, t * P:(t + 1) * P, c * 512:(c + 1) * 512],
                                 xs[:, t, c * 512:(c + 1) * 512]).then_inc(out_done, 16)
            sp.wait_ge(out_done, 16 * 4)

        @block.gpsimd
        def _(pool):
            nc.gpsimd.memset(minus_half[:, :], -0.5).then_inc(p_step, 1)
            pool.wait_ge(lo_made, 4)
            pool.dma_start(cst[:, P:], consts[:, P:]).then_inc(cst_in, 16)
            pool.dma_start(wg[:, :, :], gate_w).then_inc(wg_in, 16)
            pool.dma_start(gate_bias[:, :],
                           bass.AP(ab_gate_b.tensor, 0, [[1, N_GATES], [1, 1]])).then_inc(wg_in, 16)
            pool.dma_start(taps[:, :, :], conv_taps).then_inc(taps_in, 16)
            pool.wait_ge(p_step, 1)
            done = 0

            def rsqrt(n):
                nonlocal done
                done += 1
                pool.wait_ge(var_ready, done)
                nc.gpsimd.tensor_tensor(rstd[:, 0:n], var_eps[:, 0:n], minus_half[:, 0:n],
                                        ALU.pow).then_inc(rstd_ready, 1)

            for phase, (kind, _, _, _) in enumerate(PHASES):
                if phase:
                    pool.wait_ge(x_ready, 4 * phase)

                def norm_rows():
                    layer, i = divmod(phase, 3)
                    for j, v in enumerate((ln_g, ln_b)):
                        pool.dma_start(gb[:, j, :], v[layer, i, :].partition_broadcast(P)).then_inc(gb_in, 16)

                if kind != MIX:
                    norm_rows()
                else:
                    pool.wait_ge(acc_ready, 4 * phase)
                    for r2 in range(2):
                        for j in range(6):
                            first = (5 - r2 + j) * RPB_C + RPB_C // 2 - (GRID_W - 1)
                            pool.dma_start(rpb[64 * r2:64 * r2 + 64, :, j, :],
                                           bass.AP(na_rpb.tensor, first,
                                                   [[1, 64], [RPB_R * RPB_C, NA_H], [1, GRID_W]])
                                           ).then_inc(rpb_in, 16)
                    pool.dma_start(gn_gain[:, :], ml_gn_g[0].partition_broadcast(P)).then_inc(gn_in, 16)
                    pool.wait_ge(rpb_in, 16 * 12)
                    pool.wait_ge(cst_in, 16)
                    v = rpb[:, :, :, :].rearrange("p h j c -> p (h j) c")
                    nc.gpsimd.tensor_tensor(v, v, mask_na.unsqueeze(1).to_broadcast([P, NA_H * 6, GRID_W]),
                                            ALU.add).then_inc(rpb_made, 1)
                    pool.wait_ge(na_s_ready, NA_H)
                    norm_rows()
                    rsqrt(8)
                for t in range(NT):
                    rsqrt(1)

        @block.tensor
        def _(pe):
            mm = nc.tensor.matmul

            def split_mm(ps, s_hi, s_lo, m_hi, m_lo, first, last):
                mm(ps, s_hi, m_hi, start=first, stop=False)
                mm(ps, s_hi, m_lo, start=False, stop=False)
                return mm(ps, s_lo, m_hi, start=False, stop=last)

            def tile(slot, i):
                return w_hi[:, slot, i * 512:(i + 1) * 512], w_lo[:, slot, i * 512:(i + 1) * 512]

            def transposes(m, blocks):
                for i, b in enumerate(blocks):
                    last = nc.tensor.transpose(batch_bank(m)[:, i * P:(i + 1) * P], b, ident)
                last.then_inc(tp_ready, 1)

            def x_transposes(phase, t):
                for c in range(2):
                    m = x_batch(phase) + 2 * t + c
                    if phase == 0:
                        pe.wait_ge(x_in[m], 16)
                        pe.wait_ge(ident_in, 16)
                    else:
                        pe.wait_ge(x_ready, 4 * (phase - 1) + 2 * t + c + 1)
                    wait_batch_bank(pe, m)
                    transposes(m, [xs[:, t, (4 * c + k) * P:(4 * c + k + 1) * P] for k in range(4)])

            def natural_step(par, slots, g, after=None, new_x=None):
                for t in range(NT):
                    for c in range(2):
                        by_tile = new_x == 0 and t == 0
                        if t == 0 and not by_tile:
                            pe.wait_ge(lo_made, g + 1 + c)
                        if new_x is not None:
                            pe.wait_ge(tp_hi, x_batch(new_x) + 2 * t + c + 1)
                        ps = pair(par)[:, t, :]
                        for i in range(4):
                            hi, lo = tile(slots[c], i)
                            if by_tile:
                                if i < TILES - 1:
                                    pe.wait_ge(tile_lo, c * (TILES - 1) + i + 1)
                                else:
                                    pe.wait_ge(lo_made, c + 1)
                            mm(ps, xT_hi[:, 4 * c + i, t, :], hi, start=(c, i) == (0, 0), stop=False)
                            mm(ps, xT_hi[:, 4 * c + i, t, :], lo, start=False, stop=False)
                        if new_x is not None:
                            pe.wait_ge(tp_lo, x_batch(new_x) + 2 * t + c + 1)
                        for i in range(4):
                            hi, _ = tile(slots[c], i)
                            last = mm(ps, xT_lo[:, 4 * c + i, t, :], hi, start=False, stop=(c, i) == (1, 3))
                        if (t, c) == (1, 0):
                            last.then_inc(group_used, 1)
                        if (t, c) == (0, 1):
                            last.then_inc(proj_ready, 1)
                        if after and (t, c) != (1, 1):
                            after(2 * t + c)
                return last

            def transposed_part(ps, slot, blk, ks):
                for k in ks:
                    hi, lo = tile(slot, k % 4)
                    mm(ps, hi[:, blk], xT_hi[:, k], start=k == 0, stop=False)
                    mm(ps, hi[:, blk], xT_lo[:, k], start=False, stop=False)
                    last = mm(ps, lo[:, blk], xT_hi[:, k], start=False, stop=k == KB - 1)
                return last

            def transposed_step(par, slots, g, after=None):
                pe.wait_ge(lo_made, g + 2)
                for b in range(4):
                    for c in range(2):
                        ps = pair(par)[:, b // 2, (b % 2) * S:(b % 2 + 1) * S]
                        last = transposed_part(ps.rearrange("p (t n) -> p t n", t=NT),
                                               slots[c], slice(b * P, (b + 1) * P),
                                               range(4 * c, 4 * c + 4))
                        if (b, c) == (3, 0):
                            last.then_inc(group_used, 1)
                    if b == 1:
                        last.then_inc(proj_ready, 1)
                    if after and b < 3:
                        after(b)
                return last

            def output(phase, hi, lo, wait_pair, wait_blocks):
                g0 = GROUP0[phase] + PHASES[phase][2]
                n_groups = PHASES[phase][3] // 2
                banks = [pair(acc_pair(phase)), psum[:, 6:8, :]]

                def block_mm(j, kk, t, c):
                    kb = 2 * j + kk
                    tok = slice(t * P, (t + 1) * P)
                    w1, w2 = tile((g0 + j) % RING, 2 * kk + c)
                    return split_mm(banks[t][:, c, :], hi(kb)[:, tok], lo(kb)[:, tok], w1, w2,
                                    kb == 0, kb == 2 * n_groups - 1)

                wait_pair()
                for j in range(n_groups - 2):
                    pe.wait_ge(lo_made, g0 + j + 1)
                    wait_blocks(j)
                    for kk in range(2):
                        for t in range(NT):
                            for c in range(2):
                                last = block_mm(j, kk, t, c)
                            if (kk, t) == (1, 1):
                                last.then_inc(group_used, 1)
                for t in range(NT):
                    for c in range(2):
                        for j in range(n_groups - 2, n_groups):
                            if (t, c) == (0, 0):
                                pe.wait_ge(lo_made, g0 + j + 1)
                                wait_blocks(j)
                            for kk in range(2):
                                last = block_mm(j, kk, t, c)
                            if (t, c) == (1, 1) and j == n_groups - 2:
                                last.then_inc(group_used, 1)
                        last.then_inc(acc_ready, 1)

            def ffn(phase):
                g0, n0, m0 = GROUP0[phase], STEP0[phase], BATCH0[phase]
                f0 = sum(p[0] == FFN for p in PHASES[:phase])

                def hid_transposes():
                    pe.wait_ge(hid_ready, f0 + 1)
                    wait_batch_bank(pe, m0)
                    transposes(m0, [hid[:, t, kk * P:(kk + 1) * P] for kk in range(2) for t in range(NT)])

                def block(ps, slot, col):
                    both = ps.rearrange("p (t a n) -> p t a n", t=NT, a=2)
                    for k in range(KB):
                        c = slice(k * 256 + col, k * 256 + col + P)

                        def small_part(first, last):
                            return mm(both[:, :, 0, :], w_lo[:, slot, c], xT_hi[:, k], start=first, stop=last)

                        if k:
                            small_part(False, False)
                        last = mm(ps, w_hi[:, slot, c], xT[:, k].rearrange("p t a n -> p (t a n)"),
                                  start=k == 0, stop=k == KB - 1)
                        if k == 0:
                            small_part(False, False)
                    return last

                def four_units(it):
                    for i in range(4):
                        par = (n0 + 1 + i) % 2
                        slot = (g0 + 2 + i) % RING
                        pe.wait_ge(lo_made, it * 4 + (g0 + 3 + i))
                        if not isinstance(it, int) or i >= 2:
                            pe.wait_ge(up_sum, it * 4 + (UNITS * f0 + i - 1))
                        elif i == 1:
                            pe.wait_ge(hid_ready, f0 + 1)
                        block(pair(par)[:, 0, :], slot, 0).then_inc(proj_ready, 1)
                        if isinstance(it, int) and i == 0:
                            hid_transposes()
                        block(pair(par)[:, 1, :], slot, P).then_inc(proj_ready, 1)

                def after(q):
                    if q == 1:
                        x_transposes(phase, 1)

                x_transposes(phase, 0)
                natural_step(n0 % 2, [g0 % RING, (g0 + 1) % RING], g0, after, phase).then_inc(proj_ready, 1)
                four_units(0)
                with pe.Fori(1, UNITS // 4) as it:
                    four_units(it)

                def wait_blocks(j):
                    if j == 0:
                        pe.wait_ge(tp_lo, m0 + 1)
                    else:
                        pe.wait_ge(unit_lo, UNITS * f0 + 2 * j)

                output(phase, lambda kb: hT_hi[:, kb, :], lambda kb: hT_lo[:, kb, :],
                       lambda: pe.wait_ge(up_sum, UNITS * (f0 + 1) - 1), wait_blocks)

            def mix(phase):
                g0, n0, m0 = GROUP0[phase], STEP0[phase], BATCH0[phase]

                def step(i):
                    if i >= 2:
                        pe.wait_ge(proj_saved, i - 1)
                    slots = [(g0 + 2 * i) % RING, (g0 + 2 * i + 1) % RING]
                    args = (n0 + i) % 2, slots, g0 + 2 * i, lambda q: small_work(i, q)
                    if MIX_COLS[i] in TRANSPOSED:
                        last = transposed_step(*args)
                    else:
                        last = natural_step(*args, new_x=None if i else phase)
                    last.then_inc(proj_ready, 1)
                    small_work(i, 3)

                def gates():
                    pe.wait_ge(tp_lo, x_batch(phase) + 4)
                    pe.wait_ge(wg_split, 2)
                    for k in range(KB):
                        last = split_mm(psum[0:N_GATES, 4, 0:S].rearrange("p (t n) -> p t n", t=NT), wg_hi[:, k, :], wg_lo[:, k, :],
                                        xT_hi[:, k], xT_lo[:, k], k == 0, k == KB - 1)
                    last.then_inc(gates_ready, 1)

                def gate_transposes():
                    pe.wait_ge(gate_biased, 1)
                    for t in range(NT):
                        last = nc.tensor.transpose(psum[:, 5, t * N_GATES:(t + 1) * N_GATES],
                                                   gates_T[:, t * P:(t + 1) * P],
                                                   ident[0:N_GATES, 0:N_GATES])
                    last.then_inc(gates_ready, 1)

                def cumulate():
                    pe.wait_ge(gate_v, 2)
                    pe.wait_ge(cst_in, 16)
                    cum = psum[:, 4, 0:16].rearrange("p (t d h) -> p t d h", t=2, d=2)
                    lf = small[:, 0, :].rearrange("p (t d h) -> p t d h", t=2, d=2)
                    mm(cum[:, 0, 0, :], tri_f, lf[:, 0, 0, :], start=True, stop=True)
                    mm(cum[:, 1, 0, :], ones, lf[:, 0, 0, :], start=True, stop=False)
                    mm(cum[:, 1, 0, :], tri_f, lf[:, 1, 0, :], start=False, stop=True)
                    mm(cum[:, 1, 1, :], tri_b, lf[:, 1, 1, :], start=True, stop=True)
                    mm(cum[:, 0, 1, :], ones, lf[:, 1, 1, :], start=True, stop=False)
                    mm(cum[:, 0, 1, :], tri_b, lf[:, 0, 1, :], start=False, stop=True).then_inc(cum_ready, 1)

                def rows_of(h):
                    r = small[:, 1, :].rearrange("p (t d h) -> p t d h", t=2, d=2)
                    pe.wait_ge(gate_v, 3)
                    if h:
                        pe.wait_ge(ml_free, h)
                    for d in range(2):
                        for t in range(NT):
                            c = (2 * d + t) * P
                            last = mm(psum[:, 7, c:c + P], r[:, t, d, h:h + 1].to_broadcast([P, P]), ident,
                                      start=True, stop=True)
                    last.then_inc(row_ready, 1)

                def qk(h):
                    pe.wait_ge(proj_saved, 5)
                    if h < 2:
                        pe.wait_ge(na_max, NA_H - 1 + h)
                    else:
                        pe.wait_ge(ml_free, 4 + h - 1)
                    for t in range(NT):
                        last = mm(psum[:, score_bank(h), t * S:(t + 1) * S], q_ml[:, h, t * P:(t + 1) * P],
                                  k_ml[:, h, :], start=True, stop=True)
                    last.then_inc(ml_s_ready, 1)

                def weights_T(h):
                    pe.wait_ge(ml_p_ready, h + 1)
                    if h == 0:
                        pe.wait_ge(na_t_saved, NA_H)
                    else:
                        pe.wait_ge(ml_t_saved, h)
                    for sh in range(2):
                        for t in range(NT):
                            last = nc.tensor.transpose(psum[:, 4, (2 * sh + t) * P:(2 * sh + t + 1) * P],
                                                       score[:, h, t * S + sh * P:t * S + (sh + 1) * P], ident)
                    last.then_inc(ml_t_ready, 1)

                def pv(h):
                    pe.wait_ge(ml_t_saved, h + 1)
                    pe.wait_ge(proj_saved, 6)
                    if h == 0:
                        pe.wait_ge(ya_lo, 4)
                        pe.wait_ge(ml_free, 8)
                    if h >= 2:
                        pe.wait_ge(ml_h_saved, h - 1)
                    for t in range(NT):
                        for sh in range(2):
                            last = mm(psum[:, 6 + h % 2, t * P:(t + 1) * P],
                                      p_ml[:, h % 2, sh, t * P:(t + 1) * P],
                                      v_ml[:, sh, h * ML_D:(h + 1) * ML_D], start=sh == 0, stop=sh == 1)
                    last.then_inc(ml_h_ready, 1)

                def output_T(i):
                    pe.wait_ge(yb_ready, i + 1)
                    if i == 0:
                        pe.wait_ge(ml_t_saved, ML_H)
                    for hh in range(2):
                        for t in range(NT):
                            last = nc.tensor.transpose(psum[:, 4 + i, (2 * hh + t) * P:(2 * hh + t + 1) * P],
                                                       h_ml[:, t, (2 * i + hh) * P:(2 * i + hh + 1) * P], ident)
                    last.then_inc(yb_t_ready, 1)

                def na_scores(h):
                    blk, po = h // 2, 64 * (h % 2)
                    if h == 0:
                        pe.wait_ge(proj_saved, 3)
                    elif h == 1:
                        pe.wait_ge(ml_free, ML_H)
                    else:
                        pe.wait_ge(na_max, h - 1)
                    for t in range(NT):
                        last = mm(psum[:, score_bank(h), t * S:(t + 1) * S], q_na[po:po + 64, blk, t * P:(t + 1) * P],
                                  k_na[po:po + 64, blk, :], start=True, stop=True)
                    last.then_inc(na_s_ready, 1)

                def na_transposes(h):
                    pe.wait_ge(na_p, h + 1)
                    if h:
                        pe.wait_ge(na_t_saved, h)
                    for kh in range(2):
                        for t in range(NT):
                            last = nc.tensor.transpose(psum[:, 4, (2 * kh + t) * P:(2 * kh + t + 1) * P],
                                                       na_s[h % 3][:, t * S + kh * P:t * S + (kh + 1) * P], ident)
                    last.then_inc(na_t_ready, 1)

                def na_pv(h):
                    blk, po = h // 2, 64 * (h % 2)
                    pe.wait_ge(na_t_saved, h + 1)
                    if h % 2 == 0 and h:
                        pe.wait_ge(ya_lo, blk)
                    for kh in range(2):
                        last = mm(psum[po:po + 64, 6, 0:S], v_na[:, kh, h * NA_D:(h + 1) * NA_D],
                                  p_na[:, h % 2, kh, :], start=kh == 0, stop=kh == 1)
                    last.then_inc(na_o_ready, 1)

                def na_slot(k):
                    if 0 <= k - 3 < NA_H:
                        na_transposes(k - 3)
                    if k < NA_H:
                        na_scores(k)
                    if 0 <= k - 4 < NA_H:
                        na_pv(k - 4)

                def small_work(i, q):
                    at = 4 * i + q
                    if at == 1:
                        x_transposes(phase, 1)
                    if at == 3:
                        gates()
                    if at == 4:
                        gate_transposes()
                    if at == 6:
                        cumulate()
                    if at in ROW_QUARTERS:
                        rows_of(ROW_QUARTERS.index(at))
                    if 0 <= at - NA_QUARTER < NA_H + 4:
                        na_slot(at - NA_QUARTER)
                    if 0 <= at - QK_QUARTER < ML_H:
                        qk(at - QK_QUARTER)
                    if 0 <= at - ML_QUARTER < ML_H:
                        weights_T(at - ML_QUARTER)
                    if 0 <= at - ML_QUARTER - 1 < ML_H:
                        pv(at - ML_QUARTER - 1)

                x_transposes(phase, 0)
                for i in range(len(MIX_COLS)):
                    step(i)
                pv(ML_H - 1)

                def wait_blocks(j):
                    if j == 0:
                        pe.wait_ge(ml_h_saved, ML_H)
                    if j == 2:
                        output_T(0)
                        output_T(1)
                    if j >= 2:
                        pe.wait_ge(yb_lo, j - 1)

                output(phase, lambda kb: (yaT_hi if kb < 4 else ybT_hi)[:, kb % 4, :],
                       lambda kb: (yaT_lo if kb < 4 else ybT_lo)[:, kb % 4, :],
                       lambda: pe.wait_ge(proj_saved, 6), wait_blocks)

            def conv(phase):
                g0, n0 = GROUP0[phase], STEP0[phase]

                def second_x(q):
                    if q == 1:
                        x_transposes(phase, 1)

                def gate_transposes(b):
                    if b == 0:
                        pe.wait_ge(conv_read, 1)
                        for kb in range(4):
                            for t in range(NT):
                                last = nc.tensor.transpose(psum[:, 4 + kb // 2, (2 * (kb % 2) + t) * P:
                                                                (2 * (kb % 2) + t + 1) * P],
                                                           cg_nat[:, t, kb * P:(kb + 1) * P], ident)
                            if kb % 2:
                                last.then_inc(cg_t_ready, 1)

                x_transposes(phase, 0)
                for i in range(PHASES[phase][1]):
                    if i >= 2:
                        pe.wait_ge(conv_read, i - 1)
                    args = (n0 + i) % 2, [(g0 + 2 * i) % RING, (g0 + 2 * i + 1) % RING], g0 + 2 * i
                    if i == 0:
                        last = natural_step(*args, second_x, phase)
                    else:
                        last = transposed_step(*args, gate_transposes if i == 1 else None)
                    last.then_inc(proj_ready, 1)
                output(phase, lambda kb: zT_hi[:, kb, :], lambda kb: zT_lo[:, kb, :],
                       lambda: pe.wait_ge(conv_read, PHASES[phase][1] - 1),
                       lambda j: pe.wait_ge(z_lo, j // 2 + 1))

            for phase, (kind, _, _, _) in enumerate(PHASES):
                {FFN: ffn, MIX: mix, CONV: conv}[kind](phase)

        @block.scalar
        def _(act):
            copy = nc.scalar.copy
            act.dma_start(ident, consts[:, 0:P]).then_inc(ident_in, 16)

            counts = {"group": group_used, "proj": proj_ready, "acc": acc_ready}

            def split_hi(g, later=0):
                if g >= GROUPS:
                    return
                slot = g % RING
                act.wait_ge(raw_in[slot], later * FILL + (g // RING + 1) * FILL)
                if g >= RING:
                    which, value = USED[g - RING]
                    act.wait_ge(counts[which], later * 8 + value)
                copy(w_hi[:, slot, :], raw[:, slot, :]).then_inc(hi_made, 1)

            def batch_hi(m, dst, view):
                act.wait_ge(tp_ready, m + 1)
                copy(dst, view(batch_bank(m))).then_inc(tp_hi, 1)

            def x_in_phase(phase):
                m = x_batch(phase)
                for t in range(NT):
                    for c in range(2):
                        batch_hi(m, xT_hi[:, 4 * c:4 * c + 4, t, :],
                                 lambda b: b.rearrange("p (k n) -> p k n", k=4))
                        m += 1
                        if phase == 0 and t == 0:
                            for i in range(TILES):
                                act.wait_ge(tile_in[c * TILES + i] if i < TILES - 1 else raw_in[c], FILL)
                                copy(w_hi[:, c, tile_cols(i)], raw[:, c, tile_cols(i)]).then_inc(
                                    tile_hi if i < TILES - 1 else hi_made, 1)
                    if phase and t == 0:
                        split_hi(GROUP0[phase] - 1 + LEAD)
                if phase == 0:
                    split_hi(2)

            def scale_x():
                nc.scalar.mul(ax[:, :, :], xs[:, :, :], ALPHA).then_inc(ax_ready, 1)

            def ffn(phase):
                g0, n0, m0 = GROUP0[phase], STEP0[phase], BATCH0[phase]
                f0 = sum(p[0] == FFN for p in PHASES[:phase])

                def four_units(it):
                    for i in range(4):
                        u = it * 4 + (UNITS * f0 + i + 1)
                        ready = it * 8 + 2 * (n0 + i + 1)
                        split_hi(g0 + 5 + i, it)

                        def save_apart(b, dst):
                            act.wait_ge(proj_ready, ready + b + 1)
                            ps = pair((n0 + 1 + i) % 2)[:, b, :].rearrange("p (t a n) -> p t a n", t=NT, a=2)
                            copy(dst.rearrange("p (t n) -> p t n", t=NT), ps[:, :, 1, :]).then_inc(apart_saved, 1)

                        if not isinstance(u, int) or u > 2:
                            act.wait_ge(unit_lo, u - 2)
                        save_apart(0, unit_h[:, i % 2, :])
                        act.wait_ge(gate_sum, u)
                        nc.scalar.activation(unit_h[:, i % 2, :], unit_h[:, i % 2, :],
                                             ACT.Silu).then_inc(gate_silu, 1)
                        save_apart(1, unit_u[:, :])
                        act.wait_ge(unit_ready, u)
                        copy(hT_hi[:, bass.ds(it * 4 + (i + 2), 1), :], unit_h[:, i % 2:i % 2 + 1, :]
                             ).then_inc(unit_hi, 1)

                x_in_phase(phase)
                split_hi(g0 + LEAD)
                act.wait_ge(proj_ready, 2 * n0 + 2)
                nc.scalar.activation(hid[:, :, :], pair(n0 % 2)[:, :, 0:256], ACT.Silu).then_inc(silu_ready, 1)
                split_hi(g0 + 1 + LEAD)
                batch_hi(m0, hT_hi[:, 0:2, :], lambda b: b.rearrange("p (k n) -> p k n", k=2))
                four_units(0)
                with act.Fori(1, UNITS // 4) as it:
                    four_units(it)
                for j in range(FKB // 2 - 1):
                    split_hi(g0 + PHASES[phase][2] + j + LEAD)
                    if j == 2:
                        scale_x()
                    if j == 4 and phase == 0:
                        act.wait_ge(wg_in, 32)
                        copy(wg_hi[:, :, :], wg[:, :, :]).then_inc(wg_split, 1)

            def mix(phase):
                g0, n0, m0 = GROUP0[phase], STEP0[phase], BATCH0[phase]
                dest = {"vb": v_ml[:, :, :], "ob": o_gate[:, :, :], "va": v_na[:, :, :], "qb": q_ml[:, :, :],
                        "kb": k_ml[:, :, :], "qa": q_na, "ka": k_na}

                def evacuate(i):
                    name = MIX_COLS[i]
                    act.wait_ge(proj_ready, 2 * (n0 + i) + 2)
                    src = pair((n0 + i) % 2)
                    dst = dest[name]
                    if name in TRANSPOSED:
                        src = src.rearrange("p b (c n) -> p (b c) n", c=2)
                    if name == "ob":
                        ins = nc.scalar.activation(dst, src, ACT.Sigmoid)
                    elif name == "qa":
                        ins = nc.scalar.mul(dst, src, float(NA_D) ** -0.5)
                    elif name == "kb":
                        ins = nc.scalar.mul(dst, src, float(ML_D) ** -0.5)
                    else:
                        ins = copy(dst, src)
                    ins.then_inc(proj_saved, 1)

                def ml_exp(h):
                    act.wait_ge(max_ready, 1)
                    for d in range(2):
                        for t in range(NT):
                            lo, hi = region(d, t)
                            k = (t * 2 + d) * ML_H + h
                            v = score[:, h, lo:hi]
                            last = nc.scalar.activation(v, v, ACT.Exp, bias=small[:, 6, k:k + 1])
                    last.then_inc(ml_w_ready, 1)

                def save_ml_T(h):
                    act.wait_ge(ml_t_ready, h + 1)
                    if h >= 2:
                        act.wait_ge(ml_h_ready, h - 1)
                    copy(p_ml[:, h % 2, :, :], psum[:, 4, :].rearrange("p (a n) -> p a n", a=2)
                         ).then_inc(ml_t_saved, 1)

                def save_h(h):
                    act.wait_ge(ml_h_ready, h + 1)
                    copy(h_ml[:, :, h * P:(h + 1) * P],
                         psum[:, 6 + h % 2, 0:S].rearrange("p (t n) -> p t n", t=2)
                         ).then_inc(ml_h_saved, 1)

                def yb_parts(i):
                    act.wait_ge(yb_t_ready, i + 1)
                    copy(ybT_hi[:, 2 * i:2 * i + 2, :], psum[:, 4 + i, :].rearrange("p (k n) -> p k n", k=2)
                         ).then_inc(yb_hi, 1)

                def na_exp_of(h):
                    act.wait_ge(na_max, h + 1)
                    for t in range(NT):
                        v = na_s[h % 3][:, t * S:(t + 1) * S]
                        c = 2 * h + t
                        last = nc.scalar.activation(v, v, ACT.Exp, bias=small[:, 10, c:c + 1],
                                                    accum_out=small[:, 11, c:c + 1])
                    last.then_inc(na_exp, 1)

                def save_na_T(h):
                    act.wait_ge(na_t_ready, h + 1)
                    if h >= 2:
                        act.wait_ge(na_o_ready, h - 1)
                    copy(p_na[:, h % 2, :, :], psum[:, 4, :].rearrange("p (a n) -> p a n", a=2)
                         ).then_inc(na_t_saved, 1)

                def out_hi(blk):
                    act.wait_ge(na_o_ready, 2 * blk + 2)
                    copy(yaT_hi[:, blk, :], psum[:, 6, 0:S]).then_inc(ya_hi, 1)

                def na_slot(k):
                    if 0 <= k - 3 < NA_H:
                        save_na_T(k - 3)
                    if k < NA_H:
                        na_exp_of(k)
                    if k >= 5 and k % 2:
                        out_hi((k - 5) // 2)

                x_in_phase(phase)
                scale_x()
                split_hi(g0 + LEAD)
                split_hi(g0 + 1 + LEAD)
                for i in range(1, 7):
                    evacuate(i - 1)
                    for q in range(4):
                        if (i, q) == (1, 1):
                            act.wait_ge(gate_v, 1)
                            nc.scalar.activation(small[:, 3, :], small[:, 2, :], ACT.Exp).then_inc(gate_a, 1)
                            act.wait_ge(gate_a, 1)
                            nc.scalar.activation(small[:, 4, :], small[:, 3, :], ACT.Ln,
                                                 bias=1.0).then_inc(gate_a, 1)
                        if 0 <= 4 * i + q - NA_QUARTER < NA_H + 4:
                            na_slot(4 * i + q - NA_QUARTER)
                        if 4 * i + q - NA_QUARTER in range(ML_H):
                            ml_exp(4 * i + q - NA_QUARTER)
                        h = 4 * i + q - ML_QUARTER
                        if 0 <= h < ML_H:
                            save_ml_T(h)
                        if 0 <= h - 1 < ML_H:
                            save_h(h - 1)
                        if 4 * i + q == 20:
                            act.wait_ge(gate_v, 4)
                            nc.scalar.activation(small[:, 8, :], small[:, 7, :], ACT.Exp,
                                                 scale=-1.0).then_inc(gate_a, 1)
                        for g in splits_after(i, q):
                            split_hi(g0 + g)
                save_h(ML_H - 1)
                evacuate(6)
                g1 = g0 + 14
                split_hi(g1 + LEAD)
                for i in range(2):
                    yb_parts(i)
                split_hi(g1 + 1 + LEAD)
                split_hi(g1 + 2 + LEAD)

            def conv(phase):
                g0, n0 = GROUP0[phase], STEP0[phase]
                x_in_phase(phase)
                n_steps = PHASES[phase][1]
                for i in range(n_steps + 1):
                    if i < n_steps:
                        split_hi(g0 + 2 * i + LEAD)
                        if i == 1:
                            for b in range(2):
                                act.wait_ge(cg_t_ready, b + 1)
                                copy(cgT[:, 2 * b:2 * b + 2, :],
                                     psum[:, 4 + b, :].rearrange("p (k n) -> p k n", k=2)).then_inc(cg_saved, 1)
                        split_hi(g0 + 2 * i + 1 + LEAD)
                    if i == 0:
                        act.wait_ge(proj_ready, 2 * n0 + 2)
                        copy(cg_nat[:, :, :], pair(n0 % 2)).then_inc(conv_read, 1)
                        scale_x()
                    if i in (3, 6):
                        j = i // 3 - 1
                        act.wait_ge(conv_read, i)
                        copy(zT_hi[:, 4 * j:4 * j + 4, :], zT[:, :, :]).then_inc(z_hi, 1)
                for j in range(KB // 2 - 1):
                    split_hi(g0 + 2 * n_steps + j + LEAD)

            for phase, (kind, _, _, _) in enumerate(PHASES):
                {FFN: ffn, MIX: mix, CONV: conv}[kind](phase)

        @block.vector
        def _(dve):
            vec = nc.vector
            steps = 0

            def wait_step_result():
                dve.wait_ge(v_step, steps)

            def counted(ins):
                nonlocal steps
                steps += 1
                ins.then_inc(v_step, 1)

            def split_lo(g, slot=None):
                if isinstance(g, int):
                    if g >= GROUPS:
                        return
                    slot = g % RING
                dve.wait_ge(hi_made, g + 1)
                vec.tensor_tensor(w_lo[:, slot, :], raw[:, slot, :], w_hi[:, slot, :].bitcast(F32),
                                  ALU.subtract).then_inc(lo_made, 1)

            def batch_lo(m, hi, dst, view):
                dve.wait_ge(tp_hi, m + 1)
                vec.tensor_tensor(dst, view(batch_bank(m)), hi.bitcast(F32), ALU.subtract).then_inc(tp_lo, 1)

            def x_lo(phase, t, c):
                a = (slice(None), slice(4 * c, 4 * c + 4), t, slice(None))
                batch_lo(x_batch(phase) + 2 * t + c, xT_hi[a], xT_lo[a],
                         lambda b: b.rearrange("p (k n) -> p k n", k=4))

            rstds = 0

            def norm(phase, scale):
                banks = [pair(acc_pair(phase)), psum[:, 6:8, :]]
                dve.wait_ge(gb_in, 32 * (phase + 1))
                dve.wait_ge(ax_ready, phase + 1)

                def sums(t, c):
                    dve.wait_ge(acc_ready, 4 * phase + 2 * t + c + 1)
                    cs = slice(c * 512, (c + 1) * 512)
                    counted(vec.scalar_tensor_tensor(out=xs[:, t, cs], in0=banks[t][:, c, :], scalar=scale,
                                                     in1=ax[:, t, cs], op0=ALU.mult, op1=ALU.add))

                def half_moments(t, c):
                    wait_step_result()
                    counted(vec.bn_stats(stats[:, c, :], xs[:, t, c * 512:(c + 1) * 512]))

                def moments(t):
                    wait_step_result()
                    counted(vec.bn_aggr(mv[:, t, :], stats[:, :, :]))
                    wait_step_result()
                    vec.tensor_scalar(var_eps[:, 0:1], mv[:, t, 1:2], EPS, None, ALU.add).then_inc(var_ready, 1)

                def scaled(t):
                    nonlocal rstds
                    rstds += 1
                    for c in range(2):
                        cs = slice(c * 512, (c + 1) * 512)
                        counted(vec.scalar_tensor_tensor(out=xs[:, t, cs], in0=xs[:, t, cs],
                                                         scalar=mv[:, t, 0:1], in1=gb[:, 0, cs],
                                                         op0=ALU.subtract, op1=ALU.mult))
                    dve.wait_ge(rstd_ready, rstds)
                    for c in range(2):
                        cs = slice(c * 512, (c + 1) * 512)
                        dve.wait_ge(v_step, steps - 1 + c)
                        vec.scalar_tensor_tensor(out=xs[:, t, cs], in0=xs[:, t, cs], scalar=rstd[:, 0:1],
                                                 in1=gb[:, 1, cs], op0=ALU.mult,
                                                 op1=ALU.add).then_inc(x_ready, 1)

                for c in range(2):
                    sums(0, c)
                    half_moments(0, c)
                moments(0)
                scaled(0)
                for c in range(2):
                    sums(1, c)
                    if phase < LAST:
                        x_lo(phase + 1, 0, c)
                    half_moments(1, c)
                moments(1)
                scaled(1)
                if phase < LAST:
                    for c in range(2):
                        x_lo(phase + 1, 1, c)
                    split_lo(GROUP0[phase + 1] - 1 + LEAD)

            def ffn(phase):
                g0, n0, m0 = GROUP0[phase], STEP0[phase], BATCH0[phase]
                f0 = sum(p[0] == FFN for p in PHASES[:phase])

                def four_units(it):
                    for i in range(4):
                        u = it * 4 + (UNITS * f0 + i + 1)
                        parts = [pair((n0 + 1 + i) % 2)[:, b, :].rearrange("p (t a n) -> p t a n", t=NT, a=2)
                                 for b in range(2)]
                        h = unit_h[:, i % 2, :]
                        split_lo(it * 4 + (g0 + 4 + i), (g0 + 4 + i) % RING)
                        dve.wait_ge(apart_saved, it * 8 + (2 * UNITS * f0 + 2 * i + 1))
                        both = h.rearrange("p (t n) -> p t n", t=NT)
                        vec.tensor_tensor(both, parts[0][:, :, 0, :], both, ALU.add).then_inc(gate_sum, 1)
                        dve.wait_ge(apart_saved, it * 8 + (2 * UNITS * f0 + 2 * i + 2))
                        both = unit_u[:, :].rearrange("p (t n) -> p t n", t=NT)
                        vec.tensor_tensor(both, parts[1][:, :, 0, :], both, ALU.add).then_inc(up_sum, 1)
                        dve.wait_ge(up_sum, u)
                        dve.wait_ge(gate_silu, u)
                        vec.tensor_tensor(h, h, unit_u[:, :], ALU.mult).then_inc(unit_ready, 1)
                        dve.wait_ge(unit_hi, u)
                        kb = bass.ds(it * 4 + (i + 2), 1)
                        vec.tensor_tensor(hT_lo[:, kb, :], unit_h[:, i % 2:i % 2 + 1, :],
                                          hT_hi[:, kb, :].bitcast(F32), ALU.subtract).then_inc(unit_lo, 1)

                split_lo(g0 + LEAD)
                dve.wait_ge(silu_ready, f0 + 1)
                vec.tensor_tensor(hid[:, :, :], hid[:, :, :], pair(n0 % 2)[:, :, 256:512],
                                  ALU.mult).then_inc(hid_ready, 1)
                batch_lo(m0, hT_hi[:, 0:2, :], hT_lo[:, 0:2, :], lambda b: b.rearrange("p (k n) -> p k n", k=2))
                four_units(0)
                with dve.Fori(1, UNITS // 4) as it:
                    four_units(it)
                for j in range(-1, FKB // 2 - 1):
                    split_lo(g0 + PHASES[phase][2] + j + LEAD)
                    if j == 4 and phase == 0:
                        dve.wait_ge(wg_split, 1)
                        vec.tensor_tensor(wg_lo[:, :, :], wg[:, :, :], wg_hi[:, :, :].bitcast(F32),
                                          ALU.subtract).then_inc(wg_split, 1)
                norm(phase, 0.5)

            def mix(phase):
                nonlocal rstds
                dve.wait_ge(cst_in, 16)
                g0, n0, m0 = GROUP0[phase], STEP0[phase], BATCH0[phase]
                pre = small[:, 12:14, :]
                by = pre.rearrange("p t (d k h) -> p t d k h", d=2, k=2)
                flat = lambda row: small[:, row, :].rearrange("p (t d h) -> p t d h", t=2, d=2)

                def gate_rows():
                    dve.wait_ge(gates_ready, 2)
                    for t in range(NT):
                        counted(vec.tensor_copy(pre[:, t, :], psum[:, 5, t * N_GATES:(t + 1) * N_GATES]))
                    wait_step_result()
                    for t in range(NT):
                        f = by[:, t, :, 1, :]
                        last = vec.scalar_tensor_tensor(out=flat(2)[:, t], in0=f, scalar=-1.0, in1=f,
                                                        op0=ALU.mult, op1=ALU.min)
                    last.then_inc(gate_v, 1)

                def log_sigmoid():
                    dve.wait_ge(gate_a, 2)
                    for t in range(NT):
                        last = vec.scalar_tensor_tensor(out=flat(0)[:, t], in0=by[:, t, :, 1, :], scalar=0.0,
                                                        in1=flat(4)[:, t], op0=ALU.min, op1=ALU.subtract)
                    last.then_inc(gate_v, 1)

                def relative():
                    dve.wait_ge(cum_ready, 1)
                    counted(vec.tensor_copy(small[:, 5, :], psum[:, 4, 0:16]))
                    wait_step_result()
                    for t in range(NT):
                        last = vec.tensor_tensor(flat(1)[:, t], by[:, t, :, 0, :], flat(5)[:, t], ALU.subtract)
                    last.then_inc(gate_v, 1)

                def maxima(h):
                    dve.wait_ge(row_ready, h + 1)
                    for d in range(2):
                        for t in range(NT):
                            lo, hi = allowed(d, t)
                            r_lo, r_hi = region(d, t)
                            k = (t * 2 + d) * ML_H + h
                            mask = (mask_f if d == 0 else mask_b)
                            m_lo = mask_start(d, t)
                            last = vec.tensor_tensor_reduce(
                                score[:, h, r_lo:r_hi], psum[:, 7, d * S + lo:d * S + hi],
                                mask[:, m_lo:m_lo + hi - lo], 1.0, 0.0, ALU.add, ALU.max,
                                small[:, 14, k:k + 1])
                    last.then_inc(ml_free, 1)

                def stabilise():
                    dve.wait_ge(ml_free, 4)
                    vec.tensor_tensor(small[:, 7, :], small[:, 5, :], small[:, 14, :], ALU.add).then_inc(gate_v, 1)
                    vec.tensor_scalar(small[:, 6, :], small[:, 14, :], -1.0, None, ALU.mult).then_inc(max_ready, 1)

                def weigh(h):
                    dve.wait_ge(ml_s_ready, h + 1)
                    dve.wait_ge(ml_w_ready, h + 1)
                    for d in range(2):
                        for t in range(NT):
                            lo, hi = allowed(d, t)
                            r_lo, r_hi = region(d, t)
                            k = (t * 2 + d) * ML_H + h
                            v = score[:, h, r_lo:r_hi]
                            last = vec.tensor_tensor_reduce(
                                v, v, psum[:, score_bank(h), t * S + lo:t * S + hi], 1.0, 0.0,
                                ALU.mult, ALU.add, small[:, 15, k:k + 1])
                    last.then_inc(ml_free, 1)

                def denominators():
                    dve.wait_ge(ml_free, 8)
                    counted(vec.scalar_tensor_tensor(out=small[:, 3, :], in0=small[:, 15, :], scalar=-1.0,
                                                     in1=small[:, 15, :], op0=ALU.mult, op1=ALU.max))
                    dve.wait_ge(gate_a, 3)
                    wait_step_result()
                    counted(vec.tensor_tensor(small[:, 4, :], small[:, 3, :], small[:, 8, :], ALU.max))
                    wait_step_result()
                    counted(vec.reciprocal(small[:, 9, :], small[:, 4, :]))
                    wait_step_result()

                def combine(h):
                    for t in range(NT):
                        full, part = 1 - t, t
                        kf = (t * 2 + full) * ML_H + h
                        kp = (t * 2 + part) * ML_H + h
                        whole = score[:, h, t * S:(t + 1) * S]
                        own = score[:, h, t * S + t * P:t * S + (t + 1) * P]
                        counted(vec.tensor_scalar(whole, whole, small[:, 9, kf:kf + 1], None, ALU.mult))
                        wait_step_result()
                        last = vec.scalar_tensor_tensor(
                            out=own, in0=score[:, h, 2 * S + t * P:2 * S + (t + 1) * P],
                            scalar=small[:, 9, kp:kp + 1], in1=own, op0=ALU.mult, op1=ALU.add)
                    last.then_inc(ml_p_ready, 1)

                def rpb_keys(h, j):
                    v = rpb[:, h, j:j + ROWS, :]
                    (pitch, n), (row, _), (one, _) = v.ap
                    return bass.AP(v.tensor, v.offset + GRID_W - 1, [[pitch, n], [row, ROWS], [-one, GRID_W]])

                def na_maxima(h):
                    if h == 0:
                        dve.wait_ge(rpb_made, 1)
                    dve.wait_ge(na_s_ready, h + 1)
                    if h >= 3:
                        dve.wait_ge(na_t_ready, h - 2)
                    for t in range(NT):
                        j = 2 - 2 * t
                        c = 2 * h + t
                        counted(vec.tensor_tensor_reduce(
                            na_s[h % 3][:, t * S:(t + 1) * S].rearrange("p (j c) -> p j c", j=ROWS),
                            psum[:, score_bank(h), t * S:(t + 1) * S].rearrange("p (j c) -> p j c", j=ROWS),
                            rpb_keys(h, j), 1.0, -3e38, ALU.add, ALU.max, small[:, 12, c:c + 1]))
                    wait_step_result()
                    vec.tensor_scalar(small[:, 10, 2 * h:2 * h + 2], small[:, 12, 2 * h:2 * h + 2], -1.0, None,
                                      ALU.mult).then_inc(na_max, 1)

                def na_norm(h):
                    dve.wait_ge(na_exp, h + 1)
                    counted(vec.reciprocal(small[:, 13, 2 * h:2 * h + 2], small[:, 11, 2 * h:2 * h + 2]))
                    wait_step_result()
                    for t in range(NT):
                        v = na_s[h % 3][:, t * S:(t + 1) * S]
                        c = 2 * h + t
                        last = vec.tensor_scalar(v, v, small[:, 13, c:c + 1], None, ALU.mult)
                    last.then_inc(na_p, 1)

                def out_lo(blk):
                    dve.wait_ge(ya_hi, blk + 1)
                    vec.tensor_tensor(yaT_lo[:, blk, :], psum[:, 6, 0:S],
                                      yaT_hi[:, blk, :].bitcast(F32), ALU.subtract).then_inc(ya_lo, 1)

                def na_slot(k):
                    if k < NA_H:
                        na_maxima(k)
                    if k >= 5 and k % 2:
                        out_lo((k - 5) // 2)
                    if k < NA_H:
                        na_norm(k)

                split_lo(g0 + LEAD)
                split_lo(g0 + 1 + LEAD)
                dve.wait_ge(gates_ready, 1)
                vec.tensor_scalar(gates_T[:, :], psum[0:N_GATES, 4, 0:S], gate_bias[:, 0:1], None,
                                  ALU.add).then_inc(gate_biased, 1)
                for i in range(1, 7):
                    for q in range(4):
                        at = 4 * i + q
                        if at == 4:
                            gate_rows()
                        if at == 5:
                            log_sigmoid()
                        if at == 6:
                            relative()
                        if at in ROW_QUARTERS:
                            maxima(ROW_QUARTERS.index(at))
                        if at == ROW_QUARTERS[-1]:
                            stabilise()
                        if 0 <= at - NA_QUARTER < NA_H + 4:
                            na_slot(at - NA_QUARTER)
                        if 0 <= at - QK_QUARTER < ML_H:
                            weigh(at - QK_QUARTER)
                        if at == ML_QUARTER - 1:
                            denominators()
                        if 0 <= at - ML_QUARTER + 1 < ML_H:
                            combine(at - ML_QUARTER + 1)
                        for g in splits_after(i, q):
                            split_lo(g0 + g)

                st = norm_stats[:, :, 0:6]
                agg = norm_stats[:, :, 6:8]
                dve.wait_ge(gn_in, 16)
                dve.wait_ge(proj_saved, 7)
                for t in range(NT):
                    counted(vec.tensor_tensor(o_gate[:, t, :], o_gate[:, t, :], gn_gain[:, :], ALU.mult))
                for h in range(ML_H):
                    dve.wait_ge(ml_h_saved, h + 1)
                    for t in range(NT):
                        counted(vec.bn_stats(st[:, t * 4 + h, :], h_ml[:, t, h * P:(h + 1) * P]))
                wait_step_result()
                for i in range(8):
                    counted(vec.bn_aggr(agg[:, i, :], st[:, i, :]))
                wait_step_result()
                vec.tensor_scalar(var_eps[:, 0:8], agg[:, :, 1], EPS, None, ALU.add).then_inc(var_ready, 1)
                rstds += 1
                split_lo(g0 + 14 + LEAD)
                dve.wait_ge(rstd_ready, rstds)
                for i in range(2):
                    for h in (2 * i, 2 * i + 1):
                        for t in range(NT):
                            k = t * 4 + h
                            v = h_ml[:, t, h * P:(h + 1) * P]
                            counted(vec.tensor_scalar(v, v, agg[:, k, 0:1], rstd[:, k:k + 1],
                                                      ALU.subtract, ALU.mult))
                    wait_step_result()
                    cs = slice(2 * i * P, (2 * i + 2) * P)
                    vec.tensor_tensor(h_ml[:, :, cs], h_ml[:, :, cs], o_gate[:, :, cs],
                                      ALU.mult).then_inc(yb_ready, 1)
                for i in range(2):
                    dve.wait_ge(yb_hi, i + 1)
                    vec.tensor_tensor(ybT_lo[:, 2 * i:2 * i + 2, :],
                                      psum[:, 4 + i, :].rearrange("p (k n) -> p k n", k=2),
                                      ybT_hi[:, 2 * i:2 * i + 2, :].bitcast(F32), ALU.subtract).then_inc(yb_lo, 1)
                split_lo(g0 + 15 + LEAD)
                split_lo(g0 + 16 + LEAD)
                norm(phase, 1.0)

            def conv(phase):
                g0, n0 = GROUP0[phase], STEP0[phase]
                counted(vec.memset(uT[:, :, 0:1], 0.0))
                counted(vec.memset(uT[:, :, S + 1:S + 2], 0.0))
                split_lo(g0 + LEAD)
                split_lo(g0 + 1 + LEAD)
                dve.wait_ge(taps_in, 16)
                n_steps = PHASES[phase][1]
                for i in range(n_steps):
                    part, j = CONV_STEPS[i]
                    src = pair((n0 + i) % 2).rearrange("p b (c n) -> p (b c) n", c=2)
                    if i:
                        dve.wait_ge(proj_ready, 2 * (n0 + i) + 2)
                    if part == 1 and i:
                        vec.tensor_copy(cgT[:, :, :], src).then_inc(conv_read, 1)
                    if part == 2:
                        if i == 1:
                            dve.wait_ge(cg_saved, 2)
                        else:
                            dve.wait_ge(conv_read, i)
                        vec.tensor_tensor(uT[:, :, 1:S + 1], src, cgT[:, :, :], ALU.mult).then_inc(conv_read, 1)
                        dve.wait_ge(conv_read, i + 1)
                        wait_step_result()
                        for tap in (1, 0, 2):
                            for b in range(4):
                                w = taps[:, 4 * j + b, :]
                                u = uT[:, b, tap:tap + S]
                                if tap == 1:
                                    counted(vec.tensor_scalar(yT[:, b, :], u, w[:, 1:2], w[:, 3:4],
                                                              ALU.mult, ALU.add))
                                else:
                                    dve.wait_ge(v_step, steps - 3)
                                    counted(vec.scalar_tensor_tensor(out=yT[:, b, :], in0=u,
                                                                     scalar=w[:, tap:tap + 1], in1=yT[:, b, :],
                                                                     op0=ALU.mult, op1=ALU.add))
                    if part == 0:
                        wait_step_result()
                        if j == 1:
                            dve.wait_ge(z_hi, 1)
                        vec.tensor_tensor(zT[:, :, :], src, yT[:, :, :], ALU.mult).then_inc(conv_read, 1)
                    if i + 1 < n_steps:
                        split_lo(g0 + 2 * (i + 1) + LEAD)
                        split_lo(g0 + 2 * (i + 1) + 1 + LEAD)
                    if part == 0:
                        dve.wait_ge(z_hi, j + 1)
                        vec.tensor_tensor(zT_lo[:, 4 * j:4 * j + 4, :], zT[:, :, :],
                                          zT_hi[:, 4 * j:4 * j + 4, :].bitcast(F32),
                                          ALU.subtract).then_inc(z_lo, 1)
                for j in range(KB // 2 - 1):
                    split_lo(g0 + 2 * n_steps + j + LEAD)
                norm(phase, 1.0)

            for g, i in FIRST_TILES:
                if i == 0:
                    x_lo(0, 0, g)
                if i < TILES - 1:
                    dve.wait_ge(tile_hi, g * (TILES - 1) + i + 1)
                else:
                    dve.wait_ge(hi_made, g + 1)
                vec.tensor_tensor(w_lo[:, g, tile_cols(i)], raw[:, g, tile_cols(i)],
                                  w_hi[:, g, tile_cols(i)].bitcast(F32),
                                  ALU.subtract).then_inc(tile_lo if i < TILES - 1 else lo_made, 1)
            x_lo(0, 1, 0)
            x_lo(0, 1, 1)
            split_lo(2)
            for phase, (kind, _, _, _) in enumerate(PHASES):
                {FFN: ffn, MIX: mix, CONV: conv}[kind](phase)


_INS = ["x", "ln_g", "ln_b", "ab_gate_b", "na_rpb", "ml_gn_g"]


def weight_groups(ffn_w_in, ffn_w_out, ab_w_in, ab_w_out, sc_w_in, sc_w_out):
    groups = np.empty((GROUPS, P, TILES * 512), np.float32)
    at = 0

    def put(a):
        nonlocal at
        n = a.shape[0]
        groups[at:at + n].reshape(a.shape)[...] = a
        at += n

    def columns(w, c0):
        put(w[:, c0:c0 + 512].reshape(2, 4, P, 512).transpose(0, 2, 1, 3))

    def rows(w):
        put(w.reshape(-1, 2, P, D).transpose(0, 2, 1, 3))

    for phase, (kind, _, _, _) in enumerate(PHASES):
        layer, i = divmod(phase, 3)
        if kind == FFN:
            w = ffn_w_in[layer, i // 2].reshape(KB, P, 2, FF)
            put(w[..., :256].reshape(2, 4, P, 2, 256).transpose(0, 2, 1, 3, 4))
            put(w[..., 256:].reshape(KB, P, 2, UNITS, P).transpose(3, 1, 0, 2, 4))
            rows(ffn_w_out[layer, i // 2])
        elif kind == MIX:
            for name in MIX_COLS:
                columns(ab_w_in[0], 512 * MIX_AT[name])
            rows(ab_w_out[0])
        else:
            for part, half in CONV_STEPS:
                columns(sc_w_in[0], part * D + half * 512)
            rows(sc_w_out[0])
    return groups.reshape(GROUPS * P, TILES * 512)


def kernel(**inputs):
    import concourse.bacc as bacc
    from concourse.bass_utils import run_bass_kernel_spmd

    nc = bacc.Bacc("TRN2", target_bir_lowering=False, num_devices=1)
    given = {n: np.asarray(a) for n, a in inputs.items()}
    laid_out = {n: given[n] for n in _INS}
    laid_out["na_rpb"] = given["na_rpb"][..., ::-1]
    laid_out["weights"] = weight_groups(*[given[n] for n in (
        "ffn_w_in", "ffn_w_out", "ab_w_in", "ab_w_out", "sc_w_in", "sc_w_out")])
    laid_out["gate_w"] = given["ab_w_in"][0, :, 7 * 512:].reshape(KB, P, N_GATES).transpose(1, 0, 2)
    laid_out["conv_taps"] = np.concatenate([given["sc_conv_w"][0], given["sc_conv_b"]]).reshape(
        4, KB, P).transpose(2, 1, 0)
    laid_out["consts"] = constants()
    arrays, args = {}, []
    for name, a in laid_out.items():
        a = np.ascontiguousarray(a)
        arrays[f"in_{name}"] = a
        args.append(nc.dram_tensor(f"in_{name}", a.shape, mybir.dt.from_np(a.dtype), kind="ExternalInput").ap())
    args.append(nc.dram_tensor("out_0", (1, S, D), F32, kind="ExternalOutput").ap())
    build(nc, *args)
    r = run_bass_kernel_spmd(nc, [arrays], core_ids=[0])
    return r.results[0]["out_0"]
```
